# Optimizing a Trainium2 kernel written in Bass

```python
import jax, jax.numpy as jnp
from jax import lax
import numpy as np

D_MODEL = 1024
BATCH = 1
SEQ = 512
DEPTH = 1

CHUNK = 64
RMS_EPS = 1e-6
ROPE_BASE = 10000.0
RET_HEADS = 4
RET_V = D_MODEL // 2
RET_QK = RET_V // 2
GLA_HEADS = 4
GLA_V = D_MODEL - RET_V
GLA_QK = GLA_V // 2
GLA_GATE_RANK = 16
GLA_GATE_NORM = 16.0
MIX_WIDTH = RET_V + GLA_V
IN_SIZES = (RET_QK, RET_QK, RET_V, RET_V, GLA_QK, GLA_QK, GLA_V, GLA_V, GLA_GATE_RANK)
IN_WIDTH = sum(IN_SIZES)
D_FF = ((8 * D_MODEL // 3 + 127) // 128) * 128

kernel_name = "macaron_retention_gla_hybrid"

def rms_norm(x, g):
    xf = x.astype(jnp.float32)
    y = xf * lax.rsqrt(jnp.mean(xf * xf, axis=-1, keepdims=True) + RMS_EPS)
    return (y * g.astype(jnp.float32)).astype(x.dtype)

def swiglu(h, w_gate, w_up, w_down):
    return (jax.nn.silu(h @ w_gate) * (h @ w_up)) @ w_down

def split_heads(t, n_heads):
    b, t_len, w = t.shape
    return t.reshape(b, t_len, n_heads, w // n_heads).transpose(0, 2, 1, 3)

def merge_heads(t):
    b, h, t_len, d = t.shape
    return t.transpose(0, 2, 1, 3).reshape(b, t_len, h * d)

def rotary(t, pos):
    dk = t.shape[-1]
    half = dk // 2
    inv = ROPE_BASE ** (-jnp.arange(half, dtype=jnp.float32) * 2.0 / dk)
    ang = pos[:, None] * inv[None, :]
    cos, sin = jnp.cos(ang), jnp.sin(ang)
    t1, t2 = t[..., :half], t[..., half:]
    return jnp.concatenate([t1 * cos - t2 * sin, t1 * sin + t2 * cos], axis=-1)

def head_rms(o):
    return o * lax.rsqrt(jnp.mean(o * o, axis=-1, keepdims=True) + RMS_EPS)

def chunk_decay_attention(q, k, v, log_a):
    bsz, n_h, t_len, dk = q.shape
    n_chunks = t_len // CHUNK
    per_key = log_a.shape[-1] != 1
    qf, kf, vf = (z.astype(jnp.float32) for z in (q, k, v))
    la = log_a.astype(jnp.float32)

    def to_chunks(z):
        return z.reshape(z.shape[0], z.shape[1], n_chunks, CHUNK, z.shape[-1]).transpose(2, 0, 1, 3, 4)

    b_cum = jnp.cumsum(to_chunks(la), axis=3)
    xs = (to_chunks(qf), to_chunks(kf), to_chunks(vf), b_cum)

    def step(state, inp):
        q_c, k_c, v_c, b_c = inp
        decay = jnp.exp(-jnp.abs(b_c[..., :, None, :] - b_c[..., None, :, :]))
        if per_key:
            scores = jnp.einsum('bhik,bhjk,bhijk->bhij', q_c, k_c, decay)
        else:
            scores = jnp.einsum('bhik,bhjk->bhij', q_c, k_c) * decay[..., 0]
        out = (jnp.einsum('bhij,bhjv->bhiv', scores, v_c)
               + jnp.einsum('bhik,bhkv->bhiv', q_c * jnp.exp(b_c), state))
        b_last = b_c[..., -1:, :]
        state = (jnp.exp(b_last[..., 0, :])[..., None] * state
                 + jnp.einsum('bhjk,bhjv->bhkv', k_c * jnp.exp(b_last - b_c), v_c))
        return state, out

    s0 = jnp.zeros((bsz, n_h, dk, v.shape[-1]), jnp.float32)
    _, outs = lax.scan(step, s0, xs)
    return outs.transpose(1, 2, 0, 3, 4).reshape(bsz, n_h, t_len, v.shape[-1])

def hybrid_mixer(h, w_in, ret_norm_g, gla_w_a2, gla_b_a, gla_norm_g, w_out):
    t_len = h.shape[1]
    pos = jnp.arange(t_len, dtype=jnp.float32)
    proj = h @ w_in
    offsets = [int(o) for o in np.cumsum(IN_SIZES)[:-1]]
    (r_q, r_k, r_v, r_g, g_q, g_k, g_v, g_g, g_low) = jnp.split(proj, offsets, axis=-1)

    rdk = RET_QK // RET_HEADS
    rq = rotary(split_heads(r_q, RET_HEADS), pos)
    rk = rotary(split_heads(r_k, RET_HEADS), pos) * (rdk ** -0.5)
    rv = split_heads(r_v, RET_HEADS)
    log_gamma = jnp.log(1.0 - 2.0 ** (-5.0 - jnp.arange(RET_HEADS, dtype=jnp.float32)))
    ret_log_a = jnp.broadcast_to(log_gamma[None, :, None, None], (1, RET_HEADS, t_len, 1))
    o_ret = head_rms(chunk_decay_attention(rq, rk, rv, ret_log_a))
    o_ret = (merge_heads(o_ret) * ret_norm_g.astype(jnp.float32)).astype(h.dtype) * jax.nn.silu(r_g)

    gdk = GLA_QK // GLA_HEADS
    gq = split_heads(g_q, GLA_HEADS) * (gdk ** -0.5)
    gk = split_heads(g_k, GLA_HEADS)
    gv = split_heads(g_v, GLA_HEADS)
    gate_logit = (g_low @ gla_w_a2 + gla_b_a).astype(jnp.float32)
    gla_log_a = split_heads(jax.nn.log_sigmoid(gate_logit) / GLA_GATE_NORM, GLA_HEADS)
    o_gla = head_rms(chunk_decay_attention(gq, gk, gv, gla_log_a))
    o_gla = (merge_heads(o_gla) * gla_norm_g.astype(jnp.float32)).astype(h.dtype) * jax.nn.silu(g_g)

    return jnp.concatenate([o_ret, o_gla], axis=-1) @ w_out

def setup_inputs(seed: int = 0) -> dict:
    key = jax.random.key(seed)
    ks = jax.random.split(key, 20)
    f32 = jnp.float32

    def nrm(k, shape, fan_in):
        return jax.random.normal(k, shape, f32) * (fan_in ** -0.5)

    def gain(k, shape):
        return 1.0 + 0.02 * jax.random.normal(k, shape, f32)

    return {
        "x": jax.random.normal(ks[0], (BATCH, SEQ, D_MODEL), f32),
        "ffn1_norm_g": gain(ks[1], (DEPTH, D_MODEL)),
        "ffn1_w_gate": nrm(ks[2], (DEPTH, D_MODEL, D_FF), D_MODEL),
        "ffn1_w_up": nrm(ks[3], (DEPTH, D_MODEL, D_FF), D_MODEL),
        "ffn1_w_down": nrm(ks[4], (DEPTH, D_FF, D_MODEL), D_FF),
        "mix_norm_g": gain(ks[5], (DEPTH, D_MODEL)),
        "w_in": nrm(ks[6], (DEPTH, D_MODEL, IN_WIDTH), D_MODEL),
        "ret_norm_g": gain(ks[7], (DEPTH, RET_V)),
        "gla_w_a2": nrm(ks[8], (DEPTH, GLA_GATE_RANK, GLA_QK), GLA_GATE_RANK),
        "gla_b_a": 0.1 * jax.random.normal(ks[9], (DEPTH, GLA_QK), f32),
        "gla_norm_g": gain(ks[10], (DEPTH, GLA_V)),
        "w_out": nrm(ks[11], (DEPTH, MIX_WIDTH, D_MODEL), MIX_WIDTH),
        "ffn2_norm_g": gain(ks[12], (DEPTH, D_MODEL)),
        "ffn2_w_gate": nrm(ks[13], (DEPTH, D_MODEL, D_FF), D_MODEL),
        "ffn2_w_up": nrm(ks[14], (DEPTH, D_MODEL, D_FF), D_MODEL),
        "ffn2_w_down": nrm(ks[15], (DEPTH, D_FF, D_MODEL), D_FF),
        "final_norm_g": gain(ks[16], (D_MODEL,)),
    }

def reference(x, ffn1_norm_g, ffn1_w_gate, ffn1_w_up, ffn1_w_down, mix_norm_g, w_in,
              ret_norm_g, gla_w_a2, gla_b_a, gla_norm_g, w_out, ffn2_norm_g,
              ffn2_w_gate, ffn2_w_up, ffn2_w_down, final_norm_g):
    for l in range(DEPTH):
        x = x + 0.5 * swiglu(rms_norm(x, ffn1_norm_g[l]), ffn1_w_gate[l], ffn1_w_up[l], ffn1_w_down[l])
        x = x + hybrid_mixer(rms_norm(x, mix_norm_g[l]), w_in[l], ret_norm_g[l], gla_w_a2[l],
                             gla_b_a[l], gla_norm_g[l], w_out[l])
        x = x + 0.5 * swiglu(rms_norm(x, ffn2_norm_g[l]), ffn2_w_gate[l], ffn2_w_up[l], ffn2_w_down[l])
    return rms_norm(x, final_norm_g)


_drawn_inputs = setup_inputs


def setup_inputs(seed=0):
    import zlib

    import numpy as np

    out = dict(_drawn_inputs(seed))
    spreads = {}
    factors = {'ffn1_norm_g': 4.719,
     'ret_norm_g': 7.822,
     'gla_b_a': 3.712,
     'gla_norm_g': 7.489,
     'ffn2_norm_g': 8.0,
     'final_norm_g': 2.862}
    for name, (base, spread) in spreads.items():
        noise = np.random.default_rng([zlib.crc32(name.encode()), seed]).standard_normal(out[name].shape)
        drawn = base * np.exp(spread * noise) if base else spread * noise
        out[name] = __import__('jax').numpy.asarray(drawn.astype(out[name].dtype))
    for name, factor in factors.items():
        out[name] = (out[name] * factor).astype(out[name].dtype)
    return out
```

```python
from contextlib import ExitStack

import numpy as np
import concourse.bass as bass
from concourse import mybir

F32 = mybir.dt.float32
F32R = mybir.dt.float32r
U8 = mybir.dt.uint8
ALU = mybir.AluOpType
ACT = mybir.ActivationFunctionType
AX = mybir.AxisListType

P = 128
T = 512
NT = T // P
D = 1024
KD = D // P
DFF = 2816
PW = 256
PANEL = KD * PW
EPS = 1e-6
HALF = T // 2
CHUNKS = ((0, 1), (1, 2), (2, 4), (4, 6), (6, 8))
CHUNK = 64
HEADS = 4
DK = 64
DV = 128
RANK = 16
GATE_NORM = 16.0
GROUPS = (8, 8, 6)
LEVELS = [1 << e for e in range(9)]
NMASK = 8

RQ, RK, RV, RG, GQ, GK, GV, GG = 0, 1, 2, 4, 6, 7, 8, 10
SCORE_AT = [sum(T - P * a for a in range(j)) for j in range(NT)]
SCORES = SCORE_AT[-1] + P


def tables():
    half = DK // 2
    inv = np.float32(10000.0) ** (-np.arange(half, dtype=np.float32) * np.float32(2.0) / np.float32(DK))
    ang = np.arange(T, dtype=np.float32)[None, :] * inv[:, None].astype(np.float32)
    cos = np.tile(np.cos(ang.astype(np.float64)), (4, 1))
    sin = np.sin(ang.astype(np.float64))
    sin = np.tile(np.concatenate([-sin, sin]), (2, 1))
    rotary = np.stack([cos, sin], axis=1).astype(np.float32)
    lg = np.log(1.0 - 2.0 ** (-5.0 - np.arange(HEADS)))
    j, i = np.arange(P)[:, None], np.arange(T)[None, :]
    seen = (j // CHUNK) <= (i // CHUNK)
    decay = np.stack([np.where(seen, np.exp(np.abs(i - j) * g), 0.0) * DK ** -0.5 for g in lg], axis=1)
    j, i = np.arange(P)[:, None], np.arange(P)[None, :]
    masks = [j == i]
    for s in LEVELS[:6]:
        masks.append((j // (2 * s) == i // (2 * s)) & (j // s != i // s))
    masks.append((j < CHUNK) & (i >= CHUNK))
    return rotary, decay.astype(np.float32), np.stack(masks, axis=1).astype(np.float32)


def build(nc, a, debug=None):
    ctx = ExitStack()
    with ctx:
        def sb(name, shape, dt=F32):
            return ctx.enter_context(nc.sbuf_tensor(name, shape, dt))

        def sem(name):
            return ctx.enter_context(nc.semaphore(name))

        xT = sb("xT", [P, KD, T])
        xg_hi = sb("xg_hi", [P, KD, T], F32R)
        xg_lo = sb("xg_lo", [P, KD, T], F32R)
        w_raw = sb("w_raw", [P, 2, PANEL])
        w_hi = sb("w_hi", [P, 2, PANEL], F32R)
        w_lo = sb("w_lo", [P, 2, PANEL], F32R)
        gate_pre = sb("gate_pre", [P, 2, T])
        gate_act = sb("gate_act", [P, 2, T])
        hid = sb("hid", [P, 2, T])
        rstd = sb("rstd", [P, T])
        sq_sum = sb("sq_sum", [P, T])
        sq = sb("sq", [P, T])
        ones = sb("ones", [P, P])
        gains = sb("gains", [P, 5, KD])
        a2 = sb("a2", [2 * RANK, 2 * P])
        eps = sb("eps", [P, 1])
        warm = sb("warm", [P, 1])
        gate_bias = sb("gate_bias", [P, 2])
        masks = sb("masks", [P, NMASK, P], U8)
        low = sb("low", [2 * RANK, T])
        ident = sb("ident", [P, P])
        spread = sb("spread", [P, NT, P])
        sq_last = spread[:].rearrange("p j c -> p (j c)")
        rstd_tok = sb("rstd_tok", [P, NT])
        head_ms = sb("head_ms", [P, 2, NT, HEADS])
        hid_ctx = ExitStack()
        h_hi = hid_ctx.enter_context(nc.sbuf_tensor("h_hi", [P, KD, T], F32R))
        h_lo = hid_ctx.enter_context(nc.sbuf_tensor("h_lo", [P, KD, T], F32R))
        hid_ctx.close()
        g_qk = sb("g_qk", [P, 4, T])
        v_tok = sb("v_tok", [P, 2, NT, HEADS * DV])
        r_qk = sb("r_qk", [P, 4, T])
        scores = sb("scores", [P, HEADS * SCORES])
        o_T = sb("o_T", [P, 2 * HEADS, T])
        qk_dec = sb("qk_dec", [P, 2, 2, 2 * T])
        masks_in = scores[:, 0:NMASK * P].rearrange("p (n c) -> p n c", n=NMASK)
        o_tok = [v_tok[:, 0], qk_dec[:, 0].rearrange("p a (j c) -> p (a j) c", c=T)]
        r_scores = scores[:].rearrange("p (h c) -> p h c", h=HEADS)
        g_diag = scores[:, 0:HEADS * NT * P].rearrange("p (h j c) -> p h j c", h=HEADS, j=NT)
        g_off = scores[:, HEADS * NT * P:].rearrange("p (h c) -> p h c", h=HEADS)
        rotary = o_T[:, 0:2, :]
        swapped = o_T[:, 2:4, :]
        r_decay = o_T[:, 4:8, :]
        dec = gate_pre
        pre_sum, suf_sum = gate_act, hid

        bank = ctx.enter_context(nc.psum_tensor("bank", [P, 8, T], F32))

        x_loaded = [sem(f"x_loaded{c}") for c in range(len(CHUNKS))]
        raw_part = [sem(f"raw_part{c}") for c in range(len(CHUNKS) - 1)]
        hi_part = sem("hi_part")
        lo_part = sem("lo_part")
        gains_loaded = sem("gains_loaded")
        ident_loaded = sem("ident_loaded")
        rotary_loaded = sem("rotary_loaded")
        decay_loaded = sem("decay_loaded")
        small_loaded = sem("small_loaded")
        masks_loaded = sem("masks_loaded")
        masks_ready = sem("masks_ready")
        raw_ready = [sem(f"raw_ready{s}") for s in range(2)]
        hi_ready = sem("hi_ready")
        lo_ready = sem("lo_ready")
        tile_done = sem("tile_done")
        tile_taken = sem("tile_taken")
        ones_ready = sem("ones_ready")
        eps_ready = sem("eps_ready")
        xg_hi_ready = sem("xg_hi_ready")
        xg_lo_ready = sem("xg_lo_ready")
        sq_ready = sem("sq_ready")
        sum_ready = sem("sum_ready")
        ms_done = sem("ms_done")
        last_sq_ready = sem("last_sq_ready")
        var_ready = sem("var_ready")
        root_ready = sem("root_ready")
        rstd_tok_ready = sem("rstd_tok_ready")
        spread_ready = sem("spread_ready")
        spread_done = sem("spread_done")
        rstd_ready = sem("rstd_ready")
        first_scaled = sem("first_scaled")
        silu_ready = sem("silu_ready")
        silu_scaled = sem("silu_scaled")
        h_hi_ready = sem("h_hi_ready")
        h_ready = sem("h_ready")
        half_done = sem("half_done")
        half_added = sem("half_added")
        half_sq = sem("half_sq")
        half_sum = sem("half_sum")
        half_last_sq = sem("half_last_sq")
        half_ms = sem("half_ms")
        half_root = sem("half_root")
        half_rstd = sem("half_rstd")
        out_ready = sem("out_ready")
        out_stored = sem("out_stored")
        logits_done = sem("logits_done")
        logit_abs = sem("logit_abs")
        logit_ready = sem("logit_ready")
        logit_exp = sem("logit_exp")
        logit_ln = sem("logit_ln")
        suf_ready = sem("suf_ready")
        sums_ready = sem("sums_ready")
        dec_ready = sem("dec_ready")
        q_dec_ready = sem("q_dec_ready")
        k_dec_ready = sem("k_dec_ready")
        level_done = sem("level_done")
        level_taken = sem("level_taken")
        far_done = sem("far_done")
        far_taken = sem("far_taken")
        diag_clear = sem("diag_clear")
        swap_ready = sem("swap_ready")
        cos_part = sem("cos_part")
        sin_part = sem("sin_part")
        rot_ready = sem("rot_ready")
        rs_done = sem("rs_done")
        rs_taken = sem("rs_taken")
        av_done = sem("av_done")
        av_squared = sem("av_squared")
        sq_reduced = sem("sq_reduced")
        hvar_ready = sem("hvar_ready")
        hroot_ready = sem("hroot_ready")
        hrstd_ready = sem("hrstd_ready")
        o_normed = sem("o_normed")
        o_turned = sem("o_turned")
        o_copied = sem("o_copied")
        gate_silu = sem("gate_silu")
        o_gated = sem("o_gated")
        heads_hi_ready = sem("heads_hi_ready")
        heads_lo_ready = sem("heads_lo_ready")
        pool_lo_ready = sem("pool_lo_ready")

        first_tile = []

        def panels(count, tiles=2):
            n0 = len(first_tile)
            for _ in range(count):
                start = first_tile[-1][0] + first_tile[-1][1] if first_tile else 0
                first_tile.append((start, tiles))
            return n0

        ffn_panels = []
        FFN = {}
        for f in range(2):
            for g, hidden in enumerate(GROUPS):
                FFN[f, g] = (panels(hidden), panels(D // PW))
            if f == 0:
                LOW = panels(1, tiles=1)
                order = [GK, GQ, RQ, RK, RV, RV + 1, GV, GV + 1, RG, RG + 1, GG, GG + 1]
                PN = {}
                for w in order:
                    PN[w] = panels(1)
                WOUT = panels(D // PW)
        NPANELS = len(first_tile)

        low_slot = w_hi[:, LOW % 2, 0:KD * 2 * RANK].rearrange("p (k z c) -> p k z c", z=2, c=RANK)
        low_part = [low_slot[:, :, 0, :], low_slot[:, :, 1, :],
                    w_raw[:, LOW % 2, 0:KD * RANK].rearrange("p (k c) -> p k c", c=RANK)]

        def t_first(n):
            return first_tile[n][0]

        def t_end(n):
            return first_tile[n][0] + first_tile[n][1]

        size = [PANEL] * NPANELS
        size[LOW] = KD * RANK
        for f in range(2):
            for n in range(FFN[f, 2][1], FFN[f, 2][1] + D // PW):
                size[n] = GROUPS[2] * PW
        group_start = [0, GROUPS[0], GROUPS[0] + GROUPS[1]]
        steps_before = [0, GROUPS[0] // 2, (GROUPS[0] + GROUPS[1]) // 2]
        STEPS = DFF // PW

        def chunk_of(k):
            return next(c for c, (k0, k1) in enumerate(CHUNKS) if k0 <= k < k1)

        def x_final(norm, k):
            n0 = {1: FFN[0, 2][1], 2: WOUT, 3: FFN[1, 2][1]}[norm]
            return t_first(n0) + k + 5

        XG = {0: 0, 1: KD, 2: 2 * KD}

        block = ctx.enter_context(nc.Block())

        @block.sync
        def _(sp):
            def load(n, src, i=0):
                sp.wait_ge(lo_ready, n + 1 + 2 * i)
                sp.dma_start(w_raw[:, n % 2, 0:size[n]], src).then_inc(raw_ready[n % 2], 16)

            def ffn(f):
                gate, up, down = a[f"gate{f}"], a[f"up{f}"], a[f"down{f}"]
                for g, hidden in enumerate(GROUPS):
                    n, nd = FFN[f, g]
                    s0 = steps_before[g]
                    lo = 0
                    if f == 0 and g == 0:
                        lo = 1
                        for c, (k0, k1) in enumerate(CHUNKS):
                            last = c == len(CHUNKS) - 1
                            cols = slice(k0 * PW, k1 * PW)
                            sp.dma_start(w_raw[:, 0, cols], gate[0][:, cols])\
                              .then_inc(raw_ready[0] if last else raw_part[c], 16)
                            sp.dma_start(xT[:, k0:k1, :], a["x"][:, k0:k1, :]).then_inc(x_loaded[c], 16)
                        load(n + 1, up[0])
                        sp.dma_start(ident[:], a["ident"]).then_inc(ident_loaded, 16)
                        sp.dma_start(a2[:], a["a2"]).then_inc(small_loaded, 16)
                        sp.dma_start(gate_bias[:], a["gate_bias"]).then_inc(small_loaded, 16)
                    with sp.Fori(lo, hidden // 2) as i:
                        load(n, gate[bass.ds(i + s0, 1)].rearrange("a p c -> p (a c)"), i)
                        load(n + 1, up[bass.ds(i + s0, 1)].rearrange("a p c -> p (a c)"), i)
                    for j in range(D // PW):
                        at = group_start[g] * PW
                        load(nd + j, down[j, :, at:at + hidden * PW])

            ffn(0)
            sp.dma_start(masks_in, a["masks"]).then_inc(masks_loaded, 16)
            sp.dma_start(rotary, a["rotary"]).then_inc(rotary_loaded, 16)
            sp.dma_start(r_decay, a["decay"]).then_inc(decay_loaded, 16)
            load(LOW, a["w_low"])
            for w in order:
                load(PN[w], a["w_in"][w])
            for j in range(D // PW):
                load(WOUT + j, a["w_out"][j])
            ffn(1)
            for half in range(2):
                cols = slice(half * HALF, half * HALF + HALF)
                for k in range(0, KD, 2):
                    sp.wait_ge(out_ready, KD * half + k + 2)
                    sp.dma_start(a["out"][:, k:k + 2, cols], xT[:, k:k + 2, cols]).then_inc(out_stored, 16)
            sp.wait_ge(out_stored, 16 * KD)

        @block.gpsimd
        def _(pool):
            nc.gpsimd.memset(ones[:], 1.0).then_inc(ones_ready, 1)
            nc.gpsimd.memset(eps[:], EPS).then_inc(eps_ready, 1)

            def square(norm, k):
                if norm == 0:
                    pool.wait_ge(x_loaded[chunk_of(k)], 16)
                else:
                    pool.wait_ge(tile_taken, x_final(norm, k))
                if k == 0:
                    if norm:
                        pool.wait_ge(ms_done, norm)
                    nc.gpsimd.tensor_tensor(sq_sum[:], xT[:, 0, :], xT[:, 0, :], ALU.mult).then_inc(sum_ready, 1)
                    return
                pool.wait_ge(sum_ready, (KD - 1) * norm + k)
                nc.gpsimd.tensor_tensor(sq[:], xT[:, k, :], xT[:, k, :], ALU.mult).then_inc(sq_ready, 1)
                pool.wait_ge(sq_ready, (KD - 2) * norm + k)
                nc.gpsimd.tensor_tensor(sq_sum[:], sq_sum[:], sq[:], ALU.add).then_inc(sum_ready, 1)

            def scale_silu(c, i=0):
                for m in range(2):
                    pool.wait_ge(silu_ready, (c + i) * 2 + m + 1)
                    nc.gpsimd.tensor_tensor(gate_act[:, m, :], gate_act[:, m, :], rstd[:], ALU.mult)\
                      .then_inc(silu_scaled, 1)

            def ffn(f):
                for g, hidden in enumerate(GROUPS):
                    with pool.Fori(0, hidden // 2) as i:
                        scale_silu(f * STEPS + steps_before[g], i)

            def keys(level):
                pool.wait_ge(dec_ready, 2 * (level + 1))
                if level == 0:
                    pool.wait_ge(tile_taken, t_end(PN[GK]) + 4)
                if level >= 2:
                    pool.wait_ge(level_done, HEADS * level)
                nc.gpsimd.tensor_tensor(qk_dec[:, level % 2, 1, :], g_qk[:, 2:4, :].rearrange("p a t -> p (a t)"),
                                        dec[:].rearrange("p a t -> p (a t)"), ALU.mult).then_inc(k_dec_ready, 1)

            for k in range(KD - 1):
                square(0, k)
            ffn(0)
            pool.wait_ge(masks_loaded, 16)
            nc.gpsimd.tensor_copy(masks[:], masks_in).then_inc(masks_ready, 1)
            for k in range(KD - 1):
                square(1, k)
            for level in range(2):
                keys(level)
            pool.wait_ge(av_done, NT)
            nc.gpsimd.memset(scores[:, 0:HEADS * NT * P], 0.0).then_inc(diag_clear, 1)
            for level in range(2, len(LEVELS)):
                keys(level)
            for h in (4, 6):
                pool.wait_ge(heads_hi_ready, h + 1)
                pool.wait_ge(o_gated, 2 * HEADS)
                nc.gpsimd.tensor_tensor(h_lo[:, h, :], o_T[:, h, :], h_hi[:, h, :].bitcast(F32), ALU.subtract)\
                  .then_inc(pool_lo_ready, 1)
            for k in range(KD - 1):
                square(2, k)
            ffn(1)
            for k in range(KD - 2):
                square(3, k)
            pool.wait_ge(sum_ready, 3 * (KD - 1) + KD - 2)
            for half in range(2):
                cols = slice(half * HALF, half * HALF + HALF)
                pool.wait_ge(half_added, 2 * half + 1)
                nc.gpsimd.tensor_tensor(sq[:, cols], xT[:, KD - 2, cols], xT[:, KD - 2, cols], ALU.mult).then_inc(half_sq, 1)
                pool.wait_ge(half_sq, half + 1)
                nc.gpsimd.tensor_tensor(sq_sum[:, cols], sq_sum[:, cols], sq[:, cols], ALU.add).then_inc(half_sum, 1)

        @block.scalar
        def _(act):
            act.dma_start(gains[:], a["gains"]).then_inc(gains_loaded, 16)
            act.wait_ge(ones_ready, 1)

            def load_roots():
                nc.scalar.activation(warm[:], ones[:, 0:1], ACT.Sqrt)

            load_roots()

            def split(n, i=0):
                act.wait_ge(raw_ready[n % 2], 16 * (n // 2 + 1) + 16 * i)
                before = t_end(n - 2) if n >= 2 else 2 * n - 2
                act.wait_ge(tile_done, before + 4 + 4 * i)
                if n == LOW:
                    nc.scalar.activation(low_part[0], low_part[2], ACT.Copy).then_inc(hi_ready, 1)
                    return
                nc.scalar.activation(w_hi[:, n % 2, 0:size[n]], w_raw[:, n % 2, 0:size[n]], ACT.Copy)\
                  .then_inc(hi_ready, 1)

            def gain_hi(norm, k):
                if norm == 0:
                    act.wait_ge(x_loaded[chunk_of(k)], 16)
                else:
                    act.wait_ge(tile_taken, x_final(norm, k))
                nc.scalar.activation(xg_hi[:, k, :], xT[:, k, :], ACT.Copy, scale=gains[:, norm, k:k + 1])\
                  .then_inc(xg_hi_ready, 1)

            def square_last(norm):
                if norm == 0:
                    act.wait_ge(x_loaded[chunk_of(KD - 1)], 16)
                else:
                    act.wait_ge(tile_taken, x_final(norm, KD - 1))
                    act.wait_ge(spread_done, norm)
                nc.scalar.activation(sq_last, xT[:, KD - 1, :], ACT.Square).then_inc(last_sq_ready, 1)

            def root(norm):
                act.wait_ge(var_ready, norm + 1)
                nc.scalar.activation(rstd_tok[:], rstd_tok[:], ACT.Sqrt).then_inc(root_ready, 1)
                act.wait_ge(spread_done, norm + 1)
                nc.scalar.activation(rstd[:], bank[:, 6, :], ACT.Copy).then_inc(rstd_ready, 1)

            def gate_step(f, g, i, after, first=False):
                n = FFN[f, g][0]
                for m in range(2):
                    if first:
                        act.wait_ge(first_scaled, m + 1)
                    else:
                        act.wait_ge(tile_taken, t_first(n) + m + 5 + 4 * i)
                    nc.scalar.activation(gate_act[:, m, :], gate_pre[:, m, :], ACT.Silu).then_inc(silu_ready, 1)
                after()

            def ffn(f):
                for g, hidden in enumerate(GROUPS):
                    n, nd = FFN[f, g]
                    s0 = 0
                    if g == 0 and f == 0:
                        split(2)
                        root(0)
                        gate_step(0, 0, 0, lambda: split(3), first=True)
                        s0 = 1
                    elif g == 0:
                        root(2)
                    with act.Fori(s0, hidden // 2 - 1) as i:
                        gate_step(f, g, i, lambda: (split(n + 2, i), split(n + 3, i)))
                    gate_step(f, g, hidden // 2 - 1, lambda: (split(nd), split(nd + 1)))
                    if g == len(GROUPS) - 1:
                        load_roots()
                    for j in range(D // PW):
                        if g == len(GROUPS) - 1:
                            for m in range(2):
                                if f == 0:
                                    gain_hi(1, 2 * j + m)
                            if j == D // PW - 1 and f == 0:
                                square_last(1)
                        if nd + j + 2 < NPANELS:
                            split(nd + j + 2)

            act.wait_ge(gains_loaded, 16)
            for c, (k0, k1) in enumerate(CHUNKS):
                last = c == len(CHUNKS) - 1
                cols = slice(k0 * PW, k1 * PW)
                act.wait_ge(raw_ready[0] if last else raw_part[c], 16)
                nc.scalar.activation(w_hi[:, 0, cols], w_raw[:, 0, cols], ACT.Copy)\
                  .then_inc(hi_ready if last else hi_part, 1)
                for k in range(k0, k1):
                    gain_hi(0, k)
            square_last(0)
            split(1)
            ffn(0)

            def swap(q, c):
                act.wait_ge(tile_taken, t_first(q) + c % 2 + 5)
                if c == 0:
                    act.wait_ge(rotary_loaded, 16)
                if c >= 2:
                    act.wait_ge(rot_ready, c - 1)
                for b in range(4):
                    ins = nc.scalar.activation(swapped[32 * b:32 * b + 32, c % 2, :],
                                               r_qk[32 * (b ^ 1):32 * (b ^ 1) + 32, c, :], ACT.Copy)
                ins.then_inc(swap_ready, 1)

            def factors(level):
                s = LEVELS[level]
                act.wait_ge(sums_ready, level + 1)
                if level:
                    act.wait_ge(k_dec_ready, level)
                    act.wait_ge(q_dec_ready, level)
                for odd, src in ((0, suf_sum), (1, pre_sum)):
                    view = [z[:].rearrange("p a t -> p (a t)").rearrange("p (b o s) -> p b o s", o=2, s=s)[:, :, odd, :]
                            for z in (dec, src)]
                    nc.scalar.activation(view[0], view[1], ACT.Exp, scale=1.0 / GATE_NORM).then_inc(dec_ready, 1)

            def squares(grp, j):
                c = NT * grp + j
                act.wait_ge(av_done, c + 1)
                if c:
                    act.wait_ge(sq_reduced, c)
                nc.scalar.activation(sq[:], bank[:, 4 + j, :], ACT.Square).then_inc(av_squared, 1)
                if j == NT - 1:
                    act.wait_ge(hvar_ready, grp + 1)
                    nc.scalar.activation(head_ms[:, grp], head_ms[:, grp], ACT.Sqrt).then_inc(hroot_ready, 1)

            def silu_gate(n, *tiles):
                for m in tiles or range(2):
                    t = t_first(n) + m
                    h = t - t_first(PN[RG])
                    act.wait_ge(tile_taken, t + 5)
                    nc.scalar.activation(r_qk[:, h % 4, :], r_qk[:, h % 4, :], ACT.Silu).then_inc(gate_silu, 1)

            def heads_hi(*heads):
                for h in heads:
                    act.wait_ge(o_gated, h + 1)
                    act.wait_ge(o_turned, HEADS)
                    nc.scalar.activation(h_hi[:, h, :], o_T[:, h, :], ACT.Copy).then_inc(heads_hi_ready, 1)

            root(1)
            split(PN[GQ])
            act.wait_ge(logit_ready, 2)
            nc.scalar.activation(dec[:], pre_sum[:], ACT.Abs).then_inc(logit_abs, 1)
            act.wait_ge(logit_abs, 1)
            nc.scalar.activation(dec[:], dec[:], ACT.Exp, scale=-1.0).then_inc(logit_exp, 1)
            act.wait_ge(logit_exp, 1)
            nc.scalar.activation(dec[:], dec[:], ACT.Ln, bias=1.0).then_inc(logit_ln, 1)
            split(PN[RQ])
            factors(0)
            split(PN[RK])
            swap(PN[RQ], 0)
            swap(PN[RQ], 1)
            split(PN[RV])
            swap(PN[RK], 2)
            swap(PN[RK], 3)
            split(PN[RV + 1])
            factors(1)
            split(PN[GV])
            split(PN[GV + 1])
            factors(2)
            for j in range(NT):
                squares(0, j)
            split(PN[RG])
            for h in range(HEADS):
                act.wait_ge(o_turned, h + 1)
                nc.scalar.activation(o_T[:, h, :], bank[:, 4 + h, :], ACT.Copy).then_inc(o_copied, 1)
            split(PN[RG + 1])
            factors(3)
            factors(4)
            split(PN[GG])
            factors(5)
            factors(6)
            split(PN[GG + 1])
            act.wait_ge(tile_taken, t_end(PN[RG + 1]) + 4)
            nc.scalar.activation(r_qk[:], r_qk[:], ACT.Silu).then_inc(gate_silu, 4)
            factors(7)
            factors(8)
            split(WOUT)
            silu_gate(PN[GG])
            for level in (7, 8):
                for h in range(HEADS):
                    act.wait_ge(far_done, (level - 7) * HEADS + h + 1)
                    if level == 7:
                        for piece, at in ((0, 0), (1, 5 * P)):
                            ins = nc.scalar.activation(g_off[:, h, at:at + P], bank[:, 4 + h, piece * P:piece * P + P], ACT.Copy)
                    else:
                        ins = nc.scalar.activation(g_off[:, h, P:5 * P], bank[:, 4 + h, :], ACT.Copy)
                    ins.then_inc(far_taken, 1)
            for j in range(NT):
                squares(1, j)
            heads_hi(0, 1, 2, 3)
            silu_gate(PN[GG + 1])
            heads_hi(4, 5, 6, 7)
            split(WOUT + 1)
            for j in range(D // PW):
                gain_hi(2, 2 * j)
                gain_hi(2, 2 * j + 1)
                if j == D // PW - 1:
                    square_last(2)
                split(WOUT + j + 2)
            ffn(1)

            act.wait_ge(spread_done, 3)
            act.wait_ge(eps_ready, 1)
            for half in range(2):
                cols = slice(half * HALF, half * HALF + HALF)
                act.wait_ge(half_added, 2 * half + 2)
                nc.scalar.activation(sq_last[:, cols], xT[:, KD - 1, cols], ACT.Square).then_inc(half_last_sq, 1)
                act.wait_ge(half_ms, half + 1)
                nc.scalar.activation(rstd[:, cols], bank[:, 4 + half, 0:HALF], ACT.Sqrt, scale=1.0 / D, bias=eps[:])\
                  .then_inc(half_root, 1)

        @block.vector
        def _(dve):
            dve.sem_inc(lo_ready, 2)
            dve.sem_inc(tile_taken, 4)

            def split(n, i=0):
                dve.wait_ge(hi_ready, n + 1 + 2 * i)
                if n == LOW:
                    nc.vector.tensor_tensor(low_part[1], low_part[2], low_part[0].bitcast(F32), ALU.subtract)\
                      .then_inc(lo_ready, 1)
                    return
                nc.vector.tensor_tensor(w_lo[:, n % 2, 0:size[n]], w_raw[:, n % 2, 0:size[n]],
                                        w_hi[:, n % 2, 0:size[n]].bitcast(F32), ALU.subtract).then_inc(lo_ready, 1)

            def gain_lo(norm, k):
                dve.wait_ge(xg_hi_ready, XG[norm] + k + 1)
                nc.vector.scalar_tensor_tensor(xg_lo[:, k, :], xT[:, k, :], gains[:, norm, k:k + 1],
                                               xg_hi[:, k, :].bitcast(F32), ALU.mult, ALU.subtract)\
                  .then_inc(xg_lo_ready, 1)

            def token_rstd(norm):
                dve.wait_ge(ms_done, norm + 1)
                nc.vector.tensor_scalar(rstd_tok[:], bank[:, 7, 0:NT], 1.0 / D, EPS, ALU.mult, ALU.add).then_inc(var_ready, 1)
                dve.wait_ge(root_ready, norm + 1)
                nc.vector.reciprocal(rstd_tok[:], rstd_tok[:]).then_inc(rstd_tok_ready, 1)
                if norm == 0:
                    dve.wait_ge(ident_loaded, 16)
                dve.wait_ge(rstd_tok_ready, norm + 1)
                for j in range(NT):
                    ins = nc.vector.tensor_scalar(spread[:, j, :], ident[:], rstd_tok[:, j:j + 1], None, ALU.mult)
                ins.then_inc(spread_ready, 1)
                dve.wait_ge(rstd_ready, norm + 1)

            def gate_step(f, g, i, mid, end, first=False):
                n = FFN[f, g][0]
                t = t_first(n)
                c = f * STEPS + steps_before[g]
                for m in range(2):
                    dve.wait_ge(tile_done, t + m + 5 + 4 * i)
                    if first:
                        nc.vector.tensor_copy(gate_pre[:, m, :], bank[:, (t + m) % 4, :]).then_inc(tile_taken, 1)
                    else:
                        nc.vector.tensor_tensor(gate_pre[:, m, :], bank[:, (t + m) % 4, :], rstd[:], ALU.mult)\
                          .then_inc(tile_taken, 1)
                mid()
                if first:
                    token_rstd(0)
                    dve.wait_ge(tile_taken, t + 6)
                    for m in range(2):
                        nc.vector.tensor_tensor(gate_pre[:, m, :], gate_pre[:, m, :], rstd[:], ALU.mult)\
                          .then_inc(first_scaled, 1)
                for m in range(2):
                    dve.wait_ge(silu_scaled, (c + i) * 2 + m + 1)
                    dve.wait_ge(tile_done, t + 2 + m + 5 + 4 * i)
                    nc.vector.tensor_tensor(hid[:, m, :], bank[:, (t + 2 + m) % 4, :], gate_act[:, m, :], ALU.mult)\
                      .then_inc(tile_taken, 1)
                    to = bass.ds(i * 2 + m, 1) if not isinstance(i, int) else slice(2 * i + m, 2 * i + m + 1)
                    dve.wait_ge(tile_taken, t + 2 + m + 5 + 4 * i)
                    nc.vector.tensor_scalar(h_hi[:, to, :], hid[:, m:m + 1, :], 1.0, None, ALU.mult)\
                      .then_inc(h_hi_ready, 1)
                    dve.wait_ge(h_hi_ready, (c + i) * 2 + m + 1)
                    nc.vector.tensor_tensor(h_lo[:, to, :], hid[:, m:m + 1, :], h_hi[:, to, :].bitcast(F32),
                                            ALU.subtract).then_inc(h_ready, 1)
                end()

            def add_residual(n, m, k, factor):
                t = t_first(n) + m
                dve.wait_ge(tile_done, t + 5)
                nc.vector.scalar_tensor_tensor(xT[:, k, :], bank[:, t % 4, :], factor, xT[:, k, :],
                                               ALU.mult, ALU.add).then_inc(tile_taken, 1)

            def ffn(f):
                for g, hidden in enumerate(GROUPS):
                    n, nd = FFN[f, g]
                    s0 = 0
                    if g == 0 and f == 0:
                        gate_step(0, 0, 0, lambda: split(2), lambda: split(3), first=True)
                        s0 = 1
                    elif g == 0:
                        token_rstd(2)
                    with dve.Fori(s0, hidden // 2 - 1) as i:
                        gate_step(f, g, i, lambda: split(n + 2, i), lambda: split(n + 3, i))
                    gate_step(f, g, hidden // 2 - 1, lambda: split(nd), lambda: split(nd + 1))
                    for j in range(D // PW):
                        if nd + j == NPANELS - 1:
                            break
                        for m in range(2):
                            add_residual(nd + j, m, 2 * j + m, 0.5)
                            if g == len(GROUPS) - 1 and f == 0:
                                gain_lo(1, 2 * j + m)
                        if nd + j + 2 < NPANELS:
                            split(nd + j + 2)

            for c, (k0, k1) in enumerate(CHUNKS):
                last = c == len(CHUNKS) - 1
                cols = slice(k0 * PW, k1 * PW)
                dve.wait_ge(hi_ready if last else hi_part, 1 if last else c + 1)
                nc.vector.tensor_tensor(w_lo[:, 0, cols], w_raw[:, 0, cols], w_hi[:, 0, cols].bitcast(F32),
                                        ALU.subtract).then_inc(lo_ready if last else lo_part, 1)
                for k in range(k0, k1):
                    gain_lo(0, k)
            split(1)
            ffn(0)

            def take(n, m, out, factor=None):
                t = t_first(n) + m
                dve.wait_ge(tile_done, t + 5)
                if factor is None:
                    ins = nc.vector.tensor_tensor(out, bank[0:out.shape[0], t % 4, :], rstd[0:out.shape[0], :], ALU.mult)
                else:
                    ins = nc.vector.scalar_tensor_tensor(out, bank[:, t % 4, :], factor, rstd[:], ALU.mult, ALU.mult)
                ins.then_inc(tile_taken, 1)

            def rotate(q, c):
                dve.wait_ge(swap_ready, c + 1)
                nc.vector.tensor_tensor(r_qk[:, c, :], r_qk[:, c, :], rotary[:, 0, :], ALU.mult).then_inc(cos_part, 1)
                nc.vector.tensor_tensor(swapped[:, c % 2, :], swapped[:, c % 2, :], rotary[:, 1, :], ALU.mult)\
                  .then_inc(sin_part, 1)
                dve.wait_ge(cos_part, c + 1)
                dve.wait_ge(sin_part, c + 1)
                nc.vector.tensor_tensor(r_qk[:, c, :], r_qk[:, c, :], swapped[:, c % 2, :], ALU.add).then_inc(rot_ready, 1)

            def sums(level):
                s = LEVELS[level - 1]
                pre, suf = (z[:].rearrange("p a t -> p (a t)").rearrange("p (b o s) -> p b o s", o=2, s=s)
                            for z in (pre_sum, suf_sum))
                nb = 2 * T // (2 * s)
                dve.wait_ge(dec_ready, 2 * level)
                dve.wait_ge(sums_ready, level)
                nc.vector.tensor_tensor(suf[:, :, 0, :], suf[:, :, 0, :],
                                        pre[:, :, 1, s - 1:s].to_broadcast([P, nb, s]), ALU.add).then_inc(suf_ready, 1)
                dve.wait_ge(suf_ready, level)
                nc.vector.tensor_tensor(pre[:, :, 1, :], pre[:, :, 1, :],
                                        pre[:, :, 0, s - 1:s].to_broadcast([P, nb, s]), ALU.add).then_inc(sums_ready, 1)

            def queries(level):
                dve.wait_ge(dec_ready, 2 * (level + 1))
                if level == 0:
                    dve.wait_ge(tile_taken, t_end(PN[GQ]) + 4)
                if level >= 2:
                    dve.wait_ge(level_done, HEADS * level)
                nc.vector.tensor_tensor(qk_dec[:, level % 2, 0, :], g_qk[:, 0:2, :].rearrange("p a t -> p (a t)"),
                                        dec[:].rearrange("p a t -> p (a t)"), ALU.mult).then_inc(q_dec_ready, 1)

            def select(step):
                for h in range(HEADS):
                    dve.wait_ge(level_done, HEADS * step + h + 1)
                    if step == 0 and h == 0:
                        dve.wait_ge(diag_clear, 1)
                    nc.vector.copy_predicated(g_diag[:, h], masks[:, step:step + 1, :].to_broadcast([P, NT, P]),
                                              bank[:, 4 + h, :].rearrange("p (j c) -> p j c", j=NT))\
                      .then_inc(level_taken, 1)

            def means(grp, j):
                c = NT * grp + j
                dve.wait_ge(av_squared, c + 1)
                nc.vector.reduce_sum(head_ms[:, grp, j, :], sq[:].rearrange("p (h c) -> p h c", h=HEADS),
                                     AX.X).then_inc(sq_reduced, 1)
                if j < NT - 1:
                    return
                ms = head_ms[:, grp]
                dve.wait_ge(sq_reduced, c + 1)
                nc.vector.tensor_scalar(ms, ms, 1.0 / DV, EPS, ALU.mult, ALU.add).then_inc(hvar_ready, 1)
                dve.wait_ge(hroot_ready, grp + 1)
                nc.vector.reciprocal(ms, ms).then_inc(hrstd_ready, 1)
                dve.wait_ge(hrstd_ready, grp + 1)
                for i in range(NT):
                    nc.vector.tensor_tensor(o_tok[grp][:, i, :].rearrange("p (h c) -> p h c", h=HEADS),
                                            bank[:, 4 + i, :].rearrange("p (h c) -> p h c", h=HEADS),
                                            head_ms[:, grp, i, :].rearrange("p (h o) -> p h o", o=1).to_broadcast([P, HEADS, DV]),
                                            ALU.mult).then_inc(o_normed, 1)

            def gate_take(n, *tiles):
                for m in tiles or range(2):
                    h = t_first(n) + m - t_first(PN[RG])
                    if h == 0:
                        dve.wait_ge(rs_done, HEADS * NT)
                    if h >= 4:
                        dve.wait_ge(o_gated, h - 3)
                    take(n, m, r_qk[:, h % 4, :])

            def gate_mul(n, *tiles):
                for m in tiles or range(2):
                    h = t_first(n) + m - t_first(PN[RG])
                    dve.wait_ge(gate_silu, h + 1)
                    if h < HEADS:
                        dve.wait_ge(o_copied, h + 1)
                        o = o_T[:, h, :]
                    else:
                        dve.wait_ge(o_turned, h + 1)
                        o = bank[:, 4 + h - HEADS, :]
                    nc.vector.scalar_tensor_tensor(o_T[:, h, :], o, gains[:, 4, h:h + 1],
                                                   r_qk[:, h % 4, :], ALU.mult, ALU.mult).then_inc(o_gated, 1)

            def heads_lo(*heads):
                for h in heads:
                    dve.wait_ge(heads_hi_ready, h + 1)
                    dve.wait_ge(av_done, 2 * NT)
                    nc.vector.tensor_tensor(h_lo[:, h, :], o_T[:, h, :], h_hi[:, h, :].bitcast(F32), ALU.subtract)\
                      .then_inc(heads_lo_ready, 1)

            token_rstd(1)
            take(LOW, 0, low[:])
            split(PN[GQ])
            take(PN[GK], 0, g_qk[:, 2, :])
            take(PN[GK], 1, g_qk[:, 3, :])
            nc.vector.memset(suf_sum[:], 0.0)
            dve.wait_ge(small_loaded, 32)
            for b in range(2):
                dve.wait_ge(logits_done, b + 1)
                nc.vector.tensor_scalar(pre_sum[:, b, :], bank[:, 4 + b, :], gate_bias[:, b:b + 1], None, ALU.add)\
                  .then_inc(logit_ready, 1)
            dve.wait_ge(logit_ln, 1)
            nc.vector.scalar_tensor_tensor(pre_sum[:].rearrange("p a t -> p (a t)"), pre_sum[:].rearrange("p a t -> p (a t)"),
                                           0.0, dec[:].rearrange("p a t -> p (a t)"), ALU.min, ALU.subtract)\
              .then_inc(sums_ready, 1)
            split(PN[RQ])
            take(PN[GQ], 0, g_qk[:, 0, :], DK ** -0.5)
            take(PN[GQ], 1, g_qk[:, 1, :], DK ** -0.5)
            queries(0)
            split(PN[RK])
            sums(1)
            take(PN[RQ], 0, r_qk[:, 0, :])
            take(PN[RQ], 1, r_qk[:, 1, :])
            split(PN[RV])
            rotate(PN[RQ], 0)
            rotate(PN[RQ], 1)
            take(PN[RK], 0, r_qk[:, 2, :])
            take(PN[RK], 1, r_qk[:, 3, :])
            rotate(PN[RK], 2)
            split(PN[RV + 1])
            rotate(PN[RK], 3)

            def take_v(n, grp, part, *tiles):
                for m in tiles or range(2):
                    t = t_first(n) + m
                    dve.wait_ge(tile_done, t + 5)
                    for b in range(2):
                        j = 2 * m + b
                        ins = nc.vector.tensor_scalar(v_tok[:, grp, j, PW * part:PW * part + PW],
                                                      bank[:, t % 4, PW * b:PW * b + PW], rstd_tok[:, j:j + 1], None, ALU.mult)
                    ins.then_inc(tile_taken, 1)

            def decay_scores(*heads):
                for h in heads:
                    for j in range(NT):
                        w = T - P * j
                        dve.wait_ge(rs_done, NT * h + j + 1)
                        nc.vector.tensor_tensor(r_scores[:, h, SCORE_AT[j]:SCORE_AT[j] + w], bank[:, 4 + j, 0:w],
                                                r_decay[:, h, 0:w], ALU.mult).then_inc(rs_taken, 1)

            take_v(PN[RV], 0, 0)
            dve.wait_ge(decay_loaded, 16)
            dve.wait_ge(masks_ready, 1)
            decay_scores(0, 1)
            take_v(PN[RV + 1], 0, 1, 0)
            split(PN[GV])
            decay_scores(2, 3)
            take_v(PN[RV + 1], 0, 1, 1)
            queries(1)
            sums(2)
            split(PN[GV + 1])
            take_v(PN[GV], 1, 0, 0)
            for j in range(NT):
                means(0, j)
            take_v(PN[GV], 1, 0, 1)
            split(PN[RG])
            take_v(PN[GV + 1], 1, 1, 0)
            select(0)
            take_v(PN[GV + 1], 1, 1, 1)
            split(PN[RG + 1])
            for step, then in ((1, lambda: gate_take(PN[RG], 0)),
                               (2, lambda: (gate_take(PN[RG], 1), split(PN[GG]))),
                               (3, lambda: gate_take(PN[RG + 1], 0)),
                               (4, lambda: (gate_take(PN[RG + 1], 1), split(PN[GG + 1]))),
                               (5, lambda: (gate_mul(PN[RG]), gate_mul(PN[RG + 1]), gate_take(PN[GG], 0))),
                               (6, lambda: (gate_take(PN[GG], 1), split(WOUT))),
                               (7, lambda: gate_take(PN[GG + 1], 0))):
                select(step)
                queries(step + 1)
                if step + 2 < len(LEVELS):
                    sums(step + 2)
                then()
            for j in range(NT):
                means(1, j)
            heads_lo(0, 1, 2, 3)
            gate_take(PN[GG + 1], 1)
            gate_mul(PN[GG])
            gate_mul(PN[GG + 1])
            heads_lo(5, 7)
            split(WOUT + 1)
            for j in range(D // PW):
                for m in range(2):
                    add_residual(WOUT + j, m, 2 * j + m, 1.0)
                    gain_lo(2, 2 * j + m)
                split(WOUT + j + 2)
            ffn(1)

            def add_half(half, m):
                t = t_first(NPANELS - 1) + m
                k = KD - 2 + m
                cols = slice(half * HALF, half * HALF + HALF)
                dve.wait_ge(half_done, 2 * half + m + 1)
                nc.vector.scalar_tensor_tensor(xT[:, k, cols], bank[:, (t + 2 * half) % 4, cols], 0.5, xT[:, k, cols],
                                               ALU.mult, ALU.add).then_inc(half_added, 1)

            def half_recip(half):
                cols = slice(half * HALF, half * HALF + HALF)
                dve.wait_ge(half_root, half + 1)
                nc.vector.reciprocal(rstd[:, cols], rstd[:, cols]).then_inc(half_rstd, 1)

            def out_half(half):
                cols = slice(half * HALF, half * HALF + HALF)
                dve.wait_ge(half_rstd, half + 1)
                for k in range(KD):
                    nc.vector.scalar_tensor_tensor(xT[:, k, cols], xT[:, k, cols], gains[:, 3, k:k + 1], rstd[:, cols],
                                                   ALU.mult, ALU.mult).then_inc(out_ready, 1)

            add_half(0, 0)
            add_half(0, 1)
            add_half(1, 0)
            half_recip(0)
            add_half(1, 1)
            out_half(0)
            half_recip(1)
            out_half(1)

        @block.tensor
        def _(pe):
            pe.sem_inc(tile_done, 4)

            def tile(n, m, kt, hi, lo, fresh=None, i=0):
                t = t_first(n) + m
                pe.wait_ge(tile_taken, t + 1 + 4 * i)
                out = bank[:, t % 4, :]
                for k in range(kt):
                    at = k * PW + m * P
                    if fresh is not None:
                        pe.wait_ge(*fresh(k))
                    wh, wl = (w[:, n % 2, at:at + P] for w in (w_hi, w_lo))
                    nc.tensor.matmul(out, wh, hi[:, k, :], start=(k == 0), stop=False)
                    nc.tensor.matmul(out, wh, lo[:, k, :], start=False, stop=False)
                    ins = nc.tensor.matmul(out, wl, hi[:, k, :], start=False, stop=(k == kt - 1))
                ins.then_inc(tile_done, 1)

            def mean_square(norm):
                pe.wait_ge(sum_ready, (KD - 1) * (norm + 1))
                pe.wait_ge(last_sq_ready, norm + 1)
                if norm == 0:
                    pe.wait_ge(ones_ready, 1)
                for j in range(NT):
                    c = slice(P * j, P * j + P)
                    nc.tensor.matmul(bank[:, 7, j:j + 1], sq_sum[:, c], ones[:, 0:1], start=True, stop=False)
                    ins = nc.tensor.matmul(bank[:, 7, j:j + 1], sq_last[:, c], ones[:, 0:1], start=False, stop=True)
                ins.then_inc(ms_done, 1)

            def spread_rstd(norm):
                pe.wait_ge(spread_ready, norm + 1)
                nc.tensor.matmul(bank[:, 6, :], ones[:], spread[:].rearrange("p j c -> p (j c)"),
                                 start=True, stop=True).then_inc(spread_done, 1)

            def panel(n, kt=KD, i=0, hi=xg_hi, lo=xg_lo, fresh=None, after_first=None):
                pe.wait_ge(lo_ready, n + 3 + 2 * i)
                tile(n, 0, kt, hi, lo, fresh=fresh, i=i)
                if after_first:
                    after_first()
                tile(n, 1, kt, hi, lo, i=i)

            def first_step():
                pe.wait_ge(tile_taken, 4)
                for c, (k0, k1) in enumerate(CHUNKS):
                    last = c == len(CHUNKS) - 1
                    pe.wait_ge(lo_ready if last else lo_part, 3 if last else c + 1)
                    for k in range(k0, k1):
                        pe.wait_ge(xg_lo_ready, k + 1)
                        for m in range(2):
                            at = k * PW + m * P
                            wh, wl = (w[:, 0, at:at + P] for w in (w_hi, w_lo))
                            nc.tensor.matmul(bank[:, m, :], wh, xg_hi[:, k, :], start=(k == 0), stop=False)
                            nc.tensor.matmul(bank[:, m, :], wh, xg_lo[:, k, :], start=False, stop=False)
                            ins = nc.tensor.matmul(bank[:, m, :], wl, xg_hi[:, k, :], start=False, stop=(k == KD - 1))
                            if k == KD - 1:
                                ins.then_inc(tile_done, 1)
                panel(1, after_first=lambda: mean_square(0))
                spread_rstd(0)

            def down(n, kt, fresh):
                panel(n, kt, hi=h_hi, lo=h_lo, fresh=fresh)
                panel(n + 1, kt, hi=h_hi, lo=h_lo)
                with pe.Fori(1, D // PW // 2) as i:
                    panel(n, kt, i=i, hi=h_hi, lo=h_lo)
                    panel(n + 1, kt, i=i, hi=h_hi, lo=h_lo)

            def last_panel(n, kt):
                pe.wait_ge(lo_ready, n + 3)
                for half in range(2):
                    cols = slice(half * HALF, half * HALF + HALF)
                    for m in range(2):
                        t = t_first(n) + m
                        pe.wait_ge(tile_taken, t + 1 + 2 * half)
                        out = bank[:, (t + 2 * half) % 4, cols]
                        for k in range(kt):
                            at = k * PW + m * P
                            wh, wl = (w[:, n % 2, at:at + P] for w in (w_hi, w_lo))
                            nc.tensor.matmul(out, wh, h_hi[:, k, cols], start=(k == 0), stop=False)
                            nc.tensor.matmul(out, wh, h_lo[:, k, cols], start=False, stop=False)
                            ins = nc.tensor.matmul(out, wl, h_hi[:, k, cols], start=False, stop=(k == kt - 1))
                        ins.then_inc(half_done, 1)
                        if half == 1 and m == 0:
                            half_mean(0)
                half_mean(1)

            def half_mean(half):
                cols = slice(half * HALF, half * HALF + HALF)
                pe.wait_ge(half_sum, half + 1)
                nc.tensor.matmul(bank[:, 4 + half, 0:HALF], ones[:], sq_sum[:, cols], start=True, stop=False)
                pe.wait_ge(half_last_sq, half + 1)
                nc.tensor.matmul(bank[:, 4 + half, 0:HALF], ones[:], sq_last[:, cols], start=False, stop=True)\
                  .then_inc(half_ms, 1)

            def ffn(f):
                for g, hidden in enumerate(GROUPS):
                    n, nd = FFN[f, g]
                    s0 = 0
                    if g == 0:
                        if f == 0:
                            first_step()
                        else:
                            panel(n, fresh=lambda k: (xg_lo_ready, XG[2] + k + 1), after_first=lambda: mean_square(2))
                            spread_rstd(2)
                            panel(n + 1)
                        s0 = 1
                    with pe.Fori(s0, hidden // 2) as i:
                        panel(n, i=i)
                        panel(n + 1, i=i)
                    h_there = lambda k: (h_ready, 2 * (f * STEPS + steps_before[g]) + k + 1)
                    if nd + D // PW < NPANELS:
                        down(nd, hidden, h_there)
                    else:
                        for j in range(D // PW - 1):
                            panel(nd + j, hidden, hi=h_hi, lo=h_lo, fresh=None if j else h_there)
                        last_panel(nd + D // PW - 1, hidden)

            ffn(0)

            def panel_v(n, *tiles):
                pe.wait_ge(lo_ready, n + 3)
                for m in tiles or range(2):
                    t = t_first(n) + m
                    pe.wait_ge(tile_taken, t + 1)
                    for b in range(2):
                        tok = slice(P * (2 * m + b), P * (2 * m + b) + P)
                        out = bank[:, t % 4, PW * b:PW * b + PW]
                        for k in range(KD):
                            wh, wl = (w[:, n % 2, k * PW:k * PW + PW] for w in (w_hi, w_lo))
                            nc.tensor.matmul(out, xg_hi[:, k, tok], wh, start=(k == 0), stop=False)
                            nc.tensor.matmul(out, xg_lo[:, k, tok], wh, start=False, stop=False)
                            ins = nc.tensor.matmul(out, xg_hi[:, k, tok], wl, start=False, stop=(k == KD - 1))
                    ins.then_inc(tile_done, 1)

            def level_scores(step):
                if step:
                    pe.wait_ge(q_dec_ready, step)
                    pe.wait_ge(k_dec_ready, step)
                for h in range(HEADS):
                    rows = slice(DK * (h % 2), DK * (h % 2) + DK)
                    if step:
                        pe.wait_ge(level_taken, HEADS * (step - 1) + h + 1)
                        q, k = (qk_dec[rows, (step - 1) % 2, z, T * (h // 2):T * (h // 2) + T] for z in range(2))
                    else:
                        q, k = g_qk[rows, h // 2, :], g_qk[rows, 2 + h // 2, :]
                    for j in range(NT):
                        c = slice(P * j, P * j + P)
                        ins = nc.tensor.matmul(bank[:, 4 + h, c], k[:, c], q[:, c], start=True, stop=True)
                    ins.then_inc(level_done, 1)

            def far_scores(level):
                pe.wait_ge(q_dec_ready, level + 1)
                pe.wait_ge(k_dec_ready, level + 1)
                for h in range(HEADS):
                    rows = slice(DK * (h % 2), DK * (h % 2) + DK)
                    q, k = (qk_dec[rows, level % 2, z, T * (h // 2):T * (h // 2) + T] for z in range(2))
                    if level == 7:
                        pe.wait_ge(level_taken, HEADS * 7 + h + 1)
                        pairs = ((0, P, 2 * P), (2 * P, 3 * P, 4 * P))
                    else:
                        pe.wait_ge(far_taken, h + 1)
                        pairs = ((0, 2 * P, 4 * P), (P, 2 * P, 4 * P))
                    at = 0
                    for j0, i0, i1 in pairs:
                        ins = nc.tensor.matmul(bank[:, 4 + h, at:at + i1 - i0], k[:, j0:j0 + P], q[:, i0:i1],
                                               start=True, stop=True)
                        at += i1 - i0
                    ins.then_inc(far_done, 1)

            def retention_scores(h):
                rows = slice(DK * (h % 2), DK * (h % 2) + DK)
                for j in range(NT):
                    if h:
                        pe.wait_ge(rs_taken, NT * (h - 1) + j + 1)
                    nc.tensor.matmul(bank[:, 4 + j, 0:T - P * j], r_qk[rows, 2 + h // 2, P * j:P * j + P],
                                     r_qk[rows, h // 2, P * j:T], start=True, stop=True).then_inc(rs_done, 1)

            def outputs(grp, i):
                if grp:
                    pe.wait_ge(far_taken, 2 * HEADS)
                else:
                    pe.wait_ge(rs_taken, HEADS * NT)
                    pe.wait_ge(tile_taken, t_end(PN[RV + 1]) + 4)
                for h in range(HEADS):
                    for j in range(i + 1):
                        if grp == 0:
                            at = SCORE_AT[j] + P * (i - j)
                            score = r_scores[:, h, at:at + P]
                        elif i == j:
                            score = g_diag[:, h, j, :]
                        else:
                            at = (0, 3 * P, 5 * P)[j] + P * (i - j - 1)
                            score = g_off[:, h, at:at + P]
                        ins = nc.tensor.matmul(bank[:, 4 + i, DV * h:DV * h + DV], score,
                                               v_tok[:, grp, j, DV * h:DV * h + DV], start=(j == 0), stop=(j == i))
                ins.then_inc(av_done, 1)

            def turn(grp):
                pe.wait_ge(o_normed, NT * (grp + 1))
                for h in range(HEADS):
                    for i in range(NT):
                        ins = nc.tensor.transpose(bank[:, 4 + h, P * i:P * i + P], o_tok[grp][:, i, DV * h:DV * h + DV],
                                                  ident[:])
                    ins.then_inc(o_turned, 1)

            pe.wait_ge(lo_ready, LOW + 3)
            pe.wait_ge(tile_taken, t_first(LOW) + 1)
            for k in range(KD):
                pe.wait_ge(xg_lo_ready, XG[1] + k + 1)
                out = bank[0:2 * RANK, t_first(LOW) % 4, :]
                w = w_hi[:, LOW % 2, 2 * RANK * k:2 * RANK * (k + 1)]
                nc.tensor.matmul(out, w, xg_hi[:, k, :], start=(k == 0), stop=False)
                ins = nc.tensor.matmul(out, w, xg_lo[:, k, :], start=False, stop=(k == KD - 1))
            ins.then_inc(tile_done, 1)
            mean_square(1)
            panel(PN[GK], after_first=lambda: spread_rstd(1))
            pe.wait_ge(small_loaded, 32)
            pe.wait_ge(tile_taken, t_first(LOW) + 5)
            for b in range(2):
                nc.tensor.matmul(bank[:, 4 + b, :], a2[:, P * b:P * b + P], low[:], start=True, stop=True)\
                  .then_inc(logits_done, 1)
            panel(PN[GQ])
            panel(PN[RQ])
            panel(PN[RK])
            panel_v(PN[RV])
            panel_v(PN[RV + 1], 0)
            pe.wait_ge(rot_ready, 4)
            pe.wait_ge(logit_ready, 2)
            pe.wait_ge(rstd_ready, 2)
            retention_scores(0)
            retention_scores(1)
            panel_v(PN[RV + 1], 1)
            retention_scores(2)
            retention_scores(3)
            panel_v(PN[GV], 0)
            for i in range(NT):
                outputs(0, i)
            panel_v(PN[GV], 1)
            turn(0)
            panel_v(PN[GV + 1], 0)
            pe.wait_ge(o_copied, HEADS)
            level_scores(0)
            panel_v(PN[GV + 1], 1)
            for step, (n, m) in enumerate((n, m) for n in (PN[RG], PN[RG + 1], PN[GG], PN[GG + 1]) for m in range(2)):
                if step + 1 < NMASK:
                    level_scores(step + 1)
                else:
                    far_scores(7)
                    far_scores(8)
                    for i in range(NT):
                        outputs(1, i)
                pe.wait_ge(lo_ready, n + 3)
                tile(n, m, KD, xg_hi, xg_lo)
            turn(1)
            down(WOUT, KD, lambda k: {4: (pool_lo_ready, 1), 5: (heads_lo_ready, 5), 6: (pool_lo_ready, 2),
                                      7: (heads_lo_ready, 6)}.get(k, (heads_lo_ready, k + 1)))
            ffn(1)


def kernel(x, ffn1_norm_g, ffn1_w_gate, ffn1_w_up, ffn1_w_down, mix_norm_g, w_in, ret_norm_g, gla_w_a2, gla_b_a,
           gla_norm_g, w_out, ffn2_norm_g, ffn2_w_gate, ffn2_w_up, ffn2_w_down, final_norm_g):
    import concourse.bacc as bacc
    from concourse.bass_utils import run_bass_kernel_spmd

    def row_tiles(w):
        w = np.asarray(w)
        rows, cols = w.shape
        w = w.reshape(rows // P, P, cols // PW, PW).transpose(2, 1, 0, 3)
        return np.ascontiguousarray(w).reshape(cols // PW, P, rows // P * PW)

    def columns(v):
        return np.asarray(v).reshape(-1, P).T

    w_in = np.asarray(w_in)[0]
    wide = w_in.shape[1] - RANK
    rotary, decay, masks = tables()
    heads_g = np.concatenate([np.asarray(ret_norm_g)[0], np.asarray(gla_norm_g)[0]])
    arrays = {
        "x": np.ascontiguousarray(np.asarray(x)[0].T.reshape(KD, P, T).transpose(1, 0, 2)),
        "gate0": row_tiles(ffn1_w_gate[0]), "up0": row_tiles(ffn1_w_up[0]), "down0": row_tiles(ffn1_w_down[0]),
        "gate1": row_tiles(ffn2_w_gate[0]), "up1": row_tiles(ffn2_w_up[0]), "down1": row_tiles(ffn2_w_down[0]),
        "w_in": row_tiles(w_in[:, :wide]), "w_out": row_tiles(w_out[0]),
        "w_low": np.ascontiguousarray(w_in[:, wide:].reshape(KD, P, RANK).transpose(1, 0, 2)).reshape(P, KD * RANK),
        "gains": np.ascontiguousarray(np.stack([columns(g) for g in (
            np.asarray(ffn1_norm_g)[0], np.asarray(mix_norm_g)[0], np.asarray(ffn2_norm_g)[0],
            final_norm_g, heads_g)], axis=1)),
        "a2": np.concatenate([np.asarray(gla_w_a2)[0]] * 2),
        "gate_bias": np.ascontiguousarray(columns(np.asarray(gla_b_a)[0])),
        "ident": np.eye(P, dtype=np.float32), "rotary": rotary, "decay": decay, "masks": masks,
    }
    nc = bacc.Bacc("TRN2", target_bir_lowering=False, num_devices=1)
    handles = {n: nc.dram_tensor("in_" + n, v.shape, mybir.dt.from_np(v.dtype), kind="ExternalInput").ap()
               for n, v in arrays.items()}
    handles["out"] = nc.dram_tensor("out_xT", (P, KD, T), F32, kind="ExternalOutput").ap()
    build(nc, handles)
    r = run_bass_kernel_spmd(nc, [{"in_" + n: v for n, v in arrays.items()}], core_ids=[0])
    out = r.results[0]["out_xT"]
    return np.ascontiguousarray(out.transpose(2, 1, 0).reshape(1, T, D))
```

```python
from contextlib import ExitStack

import numpy as np
import concourse.bass as bass
from concourse import mybir

F32 = mybir.dt.float32
F32R = mybir.dt.float32r
U8 = mybir.dt.uint8
ALU = mybir.AluOpType
ACT = mybir.ActivationFunctionType
AX = mybir.AxisListType

P = 128
T = 512
NT = T // P
D = 1024
KD = D // P
DFF = 2816
PW = 256
PANEL = KD * PW
EPS = 1e-6
WARM_UP = 10
SPREAD_AT = 4
HALF = T // 2
CHUNKS = ((0, 1), (1, 2), (2, 4), (4, 6), (6, 8))
UP_CHUNKS = ((0, 4), (4, 8))
OUT_CHUNKS = (((0, 2), (2, 4), (4, 6), (6, 8)), ((0, 2), (2, 4), (4, 6), (6, 7), (7, 8)))
CHUNK = 64
HEADS = 4
DK = 64
DV = 128
RANK = 16
GATE_NORM = 16.0
GROUPS = (8, 8, 6)
LEVELS = [1 << e for e in range(9)]
NMASK = 6
DIAG_LEVELS = NMASK + 1

RQ, RK, RV, RG, GQ, GK, GV, GG = 0, 1, 2, 4, 6, 7, 8, 10
SCORE_AT = [sum(T - P * a for a in range(j)) for j in range(NT)]
SCORES = SCORE_AT[-1] + P


def tables():
    half = DK // 2
    inv = np.float32(10000.0) ** (-np.arange(half, dtype=np.float32) * np.float32(2.0) / np.float32(DK))
    ang = np.arange(T, dtype=np.float32)[None, :] * inv[:, None].astype(np.float32)
    cos = np.tile(np.cos(ang.astype(np.float64)), (4, 1))
    sin = np.sin(ang.astype(np.float64))
    sin = np.tile(np.concatenate([-sin, sin]), (2, 1))
    rotary = np.stack([cos, sin], axis=1).astype(np.float32)
    lg = np.log(1.0 - 2.0 ** (-5.0 - np.arange(HEADS)))
    j, i = np.arange(P)[:, None], np.arange(T)[None, :]
    seen = (j // CHUNK) <= (i // CHUNK)
    decay = np.stack([np.where(seen, np.exp(np.abs(i - j) * g), 0.0) * DK ** -0.5 for g in lg], axis=1)
    j, i = np.arange(P)[:, None], np.arange(P)[None, :]
    masks = []
    for s in LEVELS[:NMASK]:
        masks.append((j // (2 * s) == i // (2 * s)) & (j // s != i // s))
    return rotary, decay.astype(np.float32), np.stack(masks, axis=1).astype(np.float32)


def build(nc, a, debug=None):
    ctx = ExitStack()
    with ctx:
        def sb(name, shape, dt=F32):
            return ctx.enter_context(nc.sbuf_tensor(name, shape, dt))

        def sem(name):
            return ctx.enter_context(nc.semaphore(name))

        xT = sb("xT", [P, KD, T])
        xg_hi = sb("xg_hi", [P, KD, T], F32R)
        xg_lo = sb("xg_lo", [P, KD, T], F32R)
        w_raw = sb("w_raw", [P, 2, PANEL])
        w_hi = sb("w_hi", [P, 2, PANEL], F32R)
        w_lo = sb("w_lo", [P, 2, PANEL], F32R)
        gate_pre = sb("gate_pre", [P, 2, T])
        gate_act = sb("gate_act", [P, 2, T])
        hid = sb("hid", [P, 2, T])
        rstd = sb("rstd", [P, T])
        sq_sum = sb("sq_sum", [P, T])
        sq = sb("sq", [P, T])
        ones = sb("ones", [P, P])
        gains = sb("gains", [P, 5, KD])
        a2 = sb("a2", [2 * RANK, 2 * P])
        eps = sb("eps", [P, 1])
        warm = sb("warm", [P, 1])
        head_rows = sb("head_rows", [P, 2])
        same = sb("same", [P, NT, HEADS])
        gate_bias = sb("gate_bias", [P, 2])
        masks = sb("masks", [P, NMASK, P], U8)
        low_raw = sb("low_raw", [P, KD, RANK])
        low_split = sb("low_split", [P, KD, 2, RANK], F32R)
        low = sb("low", [2 * RANK, T])
        ident = sb("ident", [P, P])
        spread = sb("spread", [P, NT, P])
        sq_last = spread[:].rearrange("p j c -> p (j c)")
        rstd_tok = sb("rstd_tok", [P, NT])
        head_ms = sb("head_ms", [P, 2, NT, HEADS])
        hid_ctx = ExitStack()
        h_hi = hid_ctx.enter_context(nc.sbuf_tensor("h_hi", [P, KD, T], F32R))
        h_lo = hid_ctx.enter_context(nc.sbuf_tensor("h_lo", [P, KD, T], F32R))
        hid_ctx.close()
        g_qk = sb("g_qk", [P, 4, T])
        v_tok = sb("v_tok", [P, 2, NT, HEADS * DV])
        r_qk = sb("r_qk", [P, 4, T])
        scores = sb("scores", [P, HEADS * SCORES])
        o_T = sb("o_T", [P, 2 * HEADS, T])
        qk_dec = sb("qk_dec", [P, 2, 2, 2 * T])
        masks_in = scores[:, 0:NMASK * P].rearrange("p (n c) -> p n c", n=NMASK)
        o_tok = [v_tok[:, 0], qk_dec[:, 0].rearrange("p a (j c) -> p (a j) c", c=T)]
        r_scores = scores[:].rearrange("p (h c) -> p h c", h=HEADS)
        g_diag = scores[:, 0:HEADS * NT * P].rearrange("p (h j c) -> p h j c", h=HEADS, j=NT)
        g_off = scores[:, HEADS * NT * P:].rearrange("p (h c) -> p h c", h=HEADS)
        rotary = o_T[:, 0:2, :]
        qk_same = o_T[:, 0:2, :]
        swapped = o_T[:, 2:4, :]
        r_decay = o_T[:, 4:8, :]
        dec = gate_pre
        pre_sum, suf_sum = gate_act, hid

        bank = ctx.enter_context(nc.psum_tensor("bank", [P, 8, T], F32))

        x_loaded = [sem(f"x_loaded{c}") for c in range(len(CHUNKS))]
        raw_part = [sem(f"raw_part{c}") for c in range(len(CHUNKS) - 1)]
        up_raw_part = sem("up_raw_part")
        hi_part = sem("hi_part")
        lo_part = sem("lo_part")
        gains_loaded = sem("gains_loaded")
        ident_loaded = sem("ident_loaded")
        rotary_loaded = sem("rotary_loaded")
        decay_loaded = sem("decay_loaded")
        small_loaded = sem("small_loaded")
        masks_loaded = sem("masks_loaded")
        masks_ready = sem("masks_ready")
        raw_ready = [sem(f"raw_ready{s}") for s in range(2)]
        hi_ready = sem("hi_ready")
        lo_ready = sem("lo_ready")
        tile_done = sem("tile_done")
        tile_taken = sem("tile_taken")
        ones_ready = sem("ones_ready")
        eps_ready = sem("eps_ready")
        xg_hi_ready = sem("xg_hi_ready")
        xg_lo_ready = sem("xg_lo_ready")
        sq_ready = sem("sq_ready")
        sum_ready = sem("sum_ready")
        ms_done = sem("ms_done")
        last_sq_ready = sem("last_sq_ready")
        var_ready = sem("var_ready")
        root_ready = sem("root_ready")
        rstd_tok_ready = sem("rstd_tok_ready")
        spread_ready = sem("spread_ready")
        spread_done = sem("spread_done")
        rstd_ready = sem("rstd_ready")
        first_scaled = sem("first_scaled")
        silu_ready = sem("silu_ready")
        silu_scaled = sem("silu_scaled")
        h_hi_ready = sem("h_hi_ready")
        h_ready = sem("h_ready")
        half_done = sem("half_done")
        half_added = sem("half_added")
        half_sq = sem("half_sq")
        half_sum = sem("half_sum")
        half_last_sq = sem("half_last_sq")
        half_ms = sem("half_ms")
        half_root = sem("half_root")
        half_rstd = sem("half_rstd")
        half_spread = sem("half_spread")
        half_ready = sem("half_ready")
        out_ready = sem("out_ready")
        out_stored = sem("out_stored")
        low_hi_ready = sem("low_hi_ready")
        low_lo_ready = sem("low_lo_ready")
        low_done = sem("low_done")
        low_taken = sem("low_taken")
        logits_done = sem("logits_done")
        logit_abs = sem("logit_abs")
        logit_ready = sem("logit_ready")
        logit_exp = sem("logit_exp")
        logit_ln = sem("logit_ln")
        suf_ready = sem("suf_ready")
        sums_ready = sem("sums_ready")
        dec_ready = sem("dec_ready")
        q_dec_ready = sem("q_dec_ready")
        k_dec_ready = sem("k_dec_ready")
        level_done = sem("level_done")
        level_taken = sem("level_taken")
        far_done = sem("far_done")
        far_taken = sem("far_taken")
        head_rows_ready = sem("head_rows_ready")
        qk_ready = sem("qk_ready")
        same_done = sem("same_done")
        same_taken = sem("same_taken")
        same_ready = sem("same_ready")
        swap_ready = sem("swap_ready")
        cos_part = sem("cos_part")
        sin_part = sem("sin_part")
        rot_ready = sem("rot_ready")
        rs_done = sem("rs_done")
        rs_taken = sem("rs_taken")
        av_done = sem("av_done")
        av_squared = sem("av_squared")
        sq_reduced = sem("sq_reduced")
        hvar_ready = sem("hvar_ready")
        hroot_ready = sem("hroot_ready")
        hrstd_ready = sem("hrstd_ready")
        o_normed = sem("o_normed")
        o_turned = sem("o_turned")
        o_copied = sem("o_copied")
        gate_silu = sem("gate_silu")
        o_gated = sem("o_gated")
        heads_hi_ready = sem("heads_hi_ready")
        heads_lo_ready = sem("heads_lo_ready")
        pool_lo_ready = sem("pool_lo_ready")

        first_tile = []

        def panels(count):
            n0 = len(first_tile)
            for _ in range(count):
                start = first_tile[-1][0] + first_tile[-1][1] if first_tile else 0
                first_tile.append((start, 2))
            return n0

        ffn_panels = []
        FFN = {}
        for f in range(2):
            for g, hidden in enumerate(GROUPS):
                FFN[f, g] = (panels(hidden), panels(D // PW))
            if f == 0:
                order = [GK, GQ, RQ, RK, RV, RV + 1, GV, GV + 1, RG, RG + 1, GG, GG + 1]
                PN = {}
                for w in order:
                    PN[w] = panels(1)
                WOUT = panels(D // PW)
        NPANELS = len(first_tile)

        def head_slot(h):
            return (h + HEADS) % (2 * HEADS)

        def t_first(n):
            return first_tile[n][0]

        def t_end(n):
            return first_tile[n][0] + first_tile[n][1]

        size = [PANEL] * NPANELS
        for f in range(2):
            for n in range(FFN[f, 2][1], FFN[f, 2][1] + D // PW):
                size[n] = GROUPS[2] * PW
        group_start = [0, GROUPS[0], GROUPS[0] + GROUPS[1]]
        steps_before = [0, GROUPS[0] // 2, (GROUPS[0] + GROUPS[1]) // 2]
        STEPS = DFF // PW

        def chunk_of(k):
            return next(c for c, (k0, k1) in enumerate(CHUNKS) if k0 <= k < k1)

        def x_final(norm, k):
            n0 = {1: FFN[0, 2][1], 2: WOUT, 3: FFN[1, 2][1]}[norm]
            return t_first(n0) + k + 5

        XG = {0: 0, 1: KD, 2: 2 * KD}

        block = ctx.enter_context(nc.Block())

        @block.sync
        def _(sp):
            def load(n, src, i=0):
                sp.wait_ge(lo_ready, n + 1 + 2 * i)
                sp.dma_start(w_raw[:, n % 2, 0:size[n]], src).then_inc(raw_ready[n % 2], 16)

            def ffn(f):
                gate, up, down = a[f"gate{f}"], a[f"up{f}"], a[f"down{f}"]
                for g, hidden in enumerate(GROUPS):
                    n, nd = FFN[f, g]
                    s0 = steps_before[g]
                    lo = 0
                    if f == 0 and g == 0:
                        lo = 1
                        for c, (k0, k1) in enumerate(CHUNKS):
                            last = c == len(CHUNKS) - 1
                            cols = slice(k0 * PW, k1 * PW)
                            sp.dma_start(xT[:, k0:k1, :], a["x"][:, k0:k1, :]).then_inc(x_loaded[c], 16)
                            sp.dma_start(w_raw[:, 0, cols], gate[0][:, cols])\
                              .then_inc(raw_ready[0] if last else raw_part[c], 16)
                        for c, (k0, k1) in enumerate(UP_CHUNKS):
                            cols = slice(k0 * PW, k1 * PW)
                            sp.dma_start(w_raw[:, 1, cols], up[0][:, cols])\
                              .then_inc(raw_ready[1] if c else up_raw_part, 16)
                        sp.dma_start(ident[:], a["ident"]).then_inc(ident_loaded, 16)
                        sp.dma_start(low_raw[:], a["w_low"]).then_inc(small_loaded, 16)
                        sp.dma_start(a2[:], a["a2"]).then_inc(small_loaded, 16)
                        sp.dma_start(gate_bias[:], a["gate_bias"]).then_inc(small_loaded, 16)
                    with sp.Fori(lo, hidden // 2) as i:
                        load(n, gate[bass.ds(i + s0, 1)].rearrange("a p c -> p (a c)"), i)
                        load(n + 1, up[bass.ds(i + s0, 1)].rearrange("a p c -> p (a c)"), i)
                    for j in range(D // PW):
                        at = group_start[g] * PW
                        load(nd + j, down[j, :, at:at + hidden * PW])

            ffn(0)
            sp.dma_start(masks_in, a["masks"]).then_inc(masks_loaded, 16)
            sp.dma_start(rotary, a["rotary"]).then_inc(rotary_loaded, 16)
            sp.dma_start(r_decay, a["decay"]).then_inc(decay_loaded, 16)
            for w in order:
                load(PN[w], a["w_in"][w])
            for j in range(D // PW):
                load(WOUT + j, a["w_out"][j])
            ffn(1)
            for half in range(2):
                cols = slice(half * HALF, half * HALF + HALF)
                for k0, k1 in OUT_CHUNKS[half]:
                    sp.wait_ge(out_ready, KD * half + k1)
                    sp.dma_start(a["out"][:, k0:k1, cols], xT[:, k0:k1, cols]).then_inc(out_stored, 16)
            sp.wait_ge(out_stored, 16 * sum(len(chunks) for chunks in OUT_CHUNKS))

        @block.gpsimd
        def _(pool):
            nc.gpsimd.memset(ones[:], 1.0).then_inc(ones_ready, 1)
            nc.gpsimd.memset(eps[:], EPS).then_inc(eps_ready, 1)

            def square(norm, k):
                if norm == 0:
                    pool.wait_ge(x_loaded[chunk_of(k)], 16)
                else:
                    pool.wait_ge(tile_taken, x_final(norm, k))
                if k == 0:
                    if norm:
                        pool.wait_ge(ms_done, norm)
                    nc.gpsimd.tensor_tensor(sq_sum[:], xT[:, 0, :], xT[:, 0, :], ALU.mult).then_inc(sum_ready, 1)
                    return
                pool.wait_ge(sum_ready, KD * norm + k)
                nc.gpsimd.tensor_tensor(sq[:], xT[:, k, :], xT[:, k, :], ALU.mult).then_inc(sq_ready, 1)
                pool.wait_ge(sq_ready, (KD - 2) * norm + k)
                nc.gpsimd.tensor_tensor(sq_sum[:], sq_sum[:], sq[:], ALU.add).then_inc(sum_ready, 1)

            def add_last(norm):
                pool.wait_ge(last_sq_ready, norm + 1)
                pool.wait_ge(sum_ready, KD * norm + KD - 1)
                nc.gpsimd.tensor_tensor(sq_sum[:], sq_sum[:], sq_last, ALU.add).then_inc(sum_ready, 1)

            def scale_silu(c, i=0):
                for m in range(2):
                    pool.wait_ge(silu_ready, (c + i) * 2 + m + 1)
                    nc.gpsimd.tensor_tensor(gate_act[:, m, :], gate_act[:, m, :], rstd[:], ALU.mult)\
                      .then_inc(silu_scaled, 1)

            def ffn(f):
                for g, hidden in enumerate(GROUPS):
                    with pool.Fori(0, hidden // 2) as i:
                        scale_silu(f * STEPS + steps_before[g], i)

            def keys(level):
                pool.wait_ge(dec_ready, 2 * (level + 1))
                if level == 0:
                    pool.wait_ge(tile_taken, t_end(PN[GK]) + 4)
                if level >= 2:
                    pool.wait_ge(level_done, HEADS * (level - 1))
                nc.gpsimd.tensor_tensor(qk_dec[:, level % 2, 1, :], g_qk[:, 2:4, :].rearrange("p a t -> p (a t)"),
                                        dec[:].rearrange("p a t -> p (a t)"), ALU.mult).then_inc(k_dec_ready, 1)

            for k in range(KD - 1):
                square(0, k)
            add_last(0)
            ffn(0)
            pool.wait_ge(masks_loaded, 16)
            nc.gpsimd.tensor_copy(masks[:], masks_in).then_inc(masks_ready, 1)
            for k in range(KD - 1):
                square(1, k)
            add_last(1)
            for level in range(2):
                keys(level)
            pool.wait_ge(rot_ready, 4)
            nc.gpsimd.tensor_tensor(qk_same, g_qk[:, 0:2, :], g_qk[:, 2:4, :], ALU.mult).then_inc(qk_ready, 1)
            for level in range(2, len(LEVELS)):
                keys(level)
            pool.wait_ge(av_done, 2 * NT)
            for h in (0, 1, 2, 3, 4, 6):
                pool.wait_ge(heads_hi_ready, h + 1)
                nc.gpsimd.tensor_tensor(h_lo[:, h, :], o_T[:, h, :], h_hi[:, head_slot(h), :].bitcast(F32), ALU.subtract)\
                  .then_inc(pool_lo_ready, 1)
            for k in range(KD - 1):
                square(2, k)
            add_last(2)
            ffn(1)
            for k in range(KD - 2):
                square(3, k)
            pool.wait_ge(sum_ready, 3 * KD + KD - 2)
            for half in range(2):
                cols = slice(half * HALF, half * HALF + HALF)
                pool.wait_ge(half_added, 2 * half + 1)
                nc.gpsimd.tensor_tensor(sq[:, cols], xT[:, KD - 2, cols], xT[:, KD - 2, cols], ALU.mult).then_inc(half_sq, 1)
                pool.wait_ge(half_sq, half + 1)
                nc.gpsimd.tensor_tensor(sq_sum[:, cols], sq_sum[:, cols], sq[:, cols], ALU.add).then_inc(half_sum, 1)

        @block.scalar
        def _(act):
            act.dma_start(gains[:], a["gains"]).then_inc(gains_loaded, 16)
            act.wait_ge(ones_ready, 1)

            def load_roots():
                nc.scalar.activation(warm[:], ones[:, 0:1], ACT.Sqrt)

            load_roots()

            def split(n, i=0):
                act.wait_ge(raw_ready[n % 2], 16 * (n // 2 + 1) + 16 * i)
                before = t_end(n - 2) if n >= 2 else 2 * n - 2
                act.wait_ge(tile_done, before + 4 + 4 * i)
                nc.scalar.activation(w_hi[:, n % 2, 0:size[n]], w_raw[:, n % 2, 0:size[n]], ACT.Copy)\
                  .then_inc(hi_ready, 1)

            def gain_hi(norm, k):
                if norm == 0:
                    act.wait_ge(x_loaded[chunk_of(k)], 16)
                else:
                    act.wait_ge(tile_taken, x_final(norm, k))
                nc.scalar.activation(xg_hi[:, k, :], xT[:, k, :], ACT.Copy, scale=gains[:, norm, k:k + 1])\
                  .then_inc(xg_hi_ready, 1)

            def square_last(norm):
                if norm == 0:
                    act.wait_ge(x_loaded[chunk_of(KD - 1)], 16)
                else:
                    act.wait_ge(tile_taken, x_final(norm, KD - 1))
                    act.wait_ge(spread_done, norm)
                nc.scalar.activation(sq_last, xT[:, KD - 1, :], ACT.Square).then_inc(last_sq_ready, 1)

            def root(norm):
                act.wait_ge(var_ready, norm + 1)
                nc.scalar.activation(rstd_tok[:], rstd_tok[:], ACT.Sqrt).then_inc(root_ready, 1)
                act.wait_ge(spread_done, norm + 1)
                nc.scalar.activation(rstd[:], bank[:, 6, :], ACT.Copy).then_inc(rstd_ready, 1)

            def gate_step(f, g, i, after, first=False):
                n = FFN[f, g][0]
                for m in range(2):
                    if first:
                        act.wait_ge(first_scaled, m + 1)
                    else:
                        act.wait_ge(tile_taken, t_first(n) + m + 5 + 4 * i)
                    nc.scalar.activation(gate_act[:, m, :], gate_pre[:, m, :], ACT.Silu).then_inc(silu_ready, 1)
                after()

            def ffn(f):
                for g, hidden in enumerate(GROUPS):
                    n, nd = FFN[f, g]
                    s0 = 0
                    if g == 0 and f == 0:
                        split(2)
                        root(0)
                        gate_step(0, 0, 0, lambda: split(3), first=True)
                        act.wait_ge(small_loaded, 48)
                        nc.scalar.activation(low_split[:, :, 0, :], low_raw[:], ACT.Copy).then_inc(low_hi_ready, 1)
                        s0 = 1
                    elif g == 0:
                        root(2)
                    with act.Fori(s0, hidden // 2 - 1) as i:
                        gate_step(f, g, i, lambda: (split(n + 2, i), split(n + 3, i)))
                    gate_step(f, g, hidden // 2 - 1, lambda: (split(nd), split(nd + 1)))
                    if g == len(GROUPS) - 1:
                        load_roots()
                    for j in range(D // PW):
                        if g == len(GROUPS) - 1:
                            for m in range(2):
                                if f == 0:
                                    gain_hi(1, 2 * j + m)
                            if j == D // PW - 1 and f == 0:
                                square_last(1)
                        if nd + j + 2 < NPANELS and nd + j + 2 != PN[GQ]:
                            split(nd + j + 2)

            act.wait_ge(gains_loaded, 16)
            for c, (k0, k1) in enumerate(CHUNKS):
                last = c == len(CHUNKS) - 1
                cols = slice(k0 * PW, k1 * PW)
                for k in range(k0, k1):
                    gain_hi(0, k)
                act.wait_ge(raw_ready[0] if last else raw_part[c], 16)
                nc.scalar.activation(w_hi[:, 0, cols], w_raw[:, 0, cols], ACT.Copy)\
                  .then_inc(hi_ready if last else hi_part, 1)
            square_last(0)
            for c, (k0, k1) in enumerate(UP_CHUNKS):
                cols = slice(k0 * PW, k1 * PW)
                act.wait_ge(raw_ready[1] if c else up_raw_part, 16)
                nc.scalar.activation(w_hi[:, 1, cols], w_raw[:, 1, cols], ACT.Copy).then_inc(hi_ready if c else hi_part, 1)
            ffn(0)

            def swap(q, c):
                act.wait_ge(tile_taken, t_first(q) + c % 2 + 5)
                if c == 0:
                    act.wait_ge(rotary_loaded, 16)
                if c >= 2:
                    act.wait_ge(rot_ready, c - 1)
                for b in range(4):
                    ins = nc.scalar.activation(swapped[32 * b:32 * b + 32, c % 2, :],
                                               r_qk[32 * (b ^ 1):32 * (b ^ 1) + 32, c, :], ACT.Copy)
                ins.then_inc(swap_ready, 1)

            def factors(level):
                s = LEVELS[level]
                act.wait_ge(sums_ready, level + 1)
                if level:
                    act.wait_ge(k_dec_ready, level)
                    act.wait_ge(q_dec_ready, level)
                for odd, src in ((0, suf_sum), (1, pre_sum)):
                    view = [z[:].rearrange("p a t -> p (a t)").rearrange("p (b o s) -> p b o s", o=2, s=s)[:, :, odd, :]
                            for z in (dec, src)]
                    nc.scalar.activation(view[0], view[1], ACT.Exp, scale=1.0 / GATE_NORM).then_inc(dec_ready, 1)

            def squares(grp, j):
                c = NT * grp + j
                act.wait_ge(av_done, c + 1)
                if c:
                    act.wait_ge(sq_reduced, c)
                nc.scalar.activation(sq[:], bank[:, 4 + j, :], ACT.Square).then_inc(av_squared, 1)
                if j == NT - 1:
                    act.wait_ge(hvar_ready, grp + 1)
                    nc.scalar.activation(head_ms[:, grp], head_ms[:, grp], ACT.Sqrt).then_inc(hroot_ready, 1)

            def silu_gate(n, *tiles):
                for m in tiles or range(2):
                    t = t_first(n) + m
                    h = t - t_first(PN[RG])
                    act.wait_ge(tile_taken, t + 5)
                    nc.scalar.activation(r_qk[:, h % 4, :], r_qk[:, h % 4, :], ACT.Silu).then_inc(gate_silu, 1)

            def heads_hi(*heads):
                for h in heads:
                    act.wait_ge(o_gated, h + 1)
                    if h < HEADS:
                        act.wait_ge(o_turned, HEADS)
                    else:
                        act.wait_ge(k_dec_ready, len(LEVELS))
                        act.wait_ge(q_dec_ready, len(LEVELS))
                    nc.scalar.activation(h_hi[:, head_slot(h), :], o_T[:, h, :], ACT.Copy).then_inc(heads_hi_ready, 1)

            root(1)
            split(PN[GQ])
            act.wait_ge(logit_ready, 2)
            nc.scalar.activation(dec[:], pre_sum[:], ACT.Abs).then_inc(logit_abs, 1)
            split(PN[RQ])
            act.wait_ge(logit_abs, 1)
            nc.scalar.activation(dec[:], dec[:], ACT.Exp, scale=-1.0).then_inc(logit_exp, 1)
            act.wait_ge(logit_exp, 1)
            nc.scalar.activation(dec[:], dec[:], ACT.Ln, bias=1.0).then_inc(logit_ln, 1)
            factors(0)
            split(PN[RK])
            swap(PN[RQ], 0)
            swap(PN[RQ], 1)
            split(PN[RV])
            swap(PN[RK], 2)
            swap(PN[RK], 3)
            split(PN[RV + 1])
            factors(1)
            split(PN[GV])
            split(PN[GV + 1])
            factors(2)
            for j in range(NT):
                squares(0, j)
            split(PN[RG])
            for h in range(HEADS):
                act.wait_ge(o_turned, h + 1)
                nc.scalar.activation(o_T[:, h, :], bank[:, 4 + h, :], ACT.Copy).then_inc(o_copied, 1)
            split(PN[RG + 1])
            factors(3)
            factors(4)
            split(PN[GG])
            factors(5)
            factors(6)
            split(PN[GG + 1])
            act.wait_ge(tile_taken, t_end(PN[RG + 1]) + 4)
            nc.scalar.activation(r_qk[:], r_qk[:], ACT.Silu).then_inc(gate_silu, 4)
            factors(7)
            heads_hi(0, 1, 2, 3)
            factors(8)
            split(WOUT)
            silu_gate(PN[GG])
            for level in (7, 8):
                for h in range(HEADS):
                    act.wait_ge(far_done, (level - 7) * HEADS + h + 1)
                    if level == 7:
                        for piece, at in ((0, 0), (1, 5 * P)):
                            ins = nc.scalar.activation(g_off[:, h, at:at + P], bank[:, 4 + h, piece * P:piece * P + P], ACT.Copy)
                    else:
                        ins = nc.scalar.activation(g_off[:, h, P:5 * P], bank[:, 4 + h, :], ACT.Copy)
                    ins.then_inc(far_taken, 1)
            for j in range(NT):
                squares(1, j)
            silu_gate(PN[GG + 1], 0)
            split(WOUT + 1)
            silu_gate(PN[GG + 1], 1)
            heads_hi(4, 5, 6, 7)
            for j in range(D // PW):
                gain_hi(2, 2 * j)
                gain_hi(2, 2 * j + 1)
                if j == D // PW - 1:
                    square_last(2)
                split(WOUT + j + 2)
            ffn(1)

            act.wait_ge(spread_done, 3)
            act.wait_ge(eps_ready, 1)
            for half in range(2):
                cols = slice(half * HALF, half * HALF + HALF)
                act.wait_ge(half_added, 2 * half + 2)
                nc.scalar.activation(sq_last[:, cols], xT[:, KD - 1, cols], ACT.Square).then_inc(half_last_sq, 1)
                act.wait_ge(half_ms, half + 1)
                nc.scalar.activation(rstd_tok[:, 2 * half:2 * half + 2], bank[:, 6:8, half], ACT.Sqrt,
                                     scale=1.0 / D, bias=eps[:]).then_inc(half_root, 1)

        @block.vector
        def _(dve):
            dve.sem_inc(lo_ready, 2)
            dve.sem_inc(tile_taken, 4)
            for h in range(2):
                for z in range(2):
                    nc.vector.memset(head_rows[DK * h:DK * h + DK, z:z + 1], float(h == z)).then_inc(head_rows_ready, 1)

            def split(n, i=0):
                dve.wait_ge(hi_ready, n + 1 + 2 * i)
                nc.vector.tensor_tensor(w_lo[:, n % 2, 0:size[n]], w_raw[:, n % 2, 0:size[n]],
                                        w_hi[:, n % 2, 0:size[n]].bitcast(F32), ALU.subtract).then_inc(lo_ready, 1)

            def gain_lo(norm, k):
                dve.wait_ge(xg_hi_ready, XG[norm] + k + 1)
                nc.vector.scalar_tensor_tensor(xg_lo[:, k, :], xT[:, k, :], gains[:, norm, k:k + 1],
                                               xg_hi[:, k, :].bitcast(F32), ALU.mult, ALU.subtract)\
                  .then_inc(xg_lo_ready, 1)

            def token_rstd(norm):
                dve.wait_ge(ms_done, norm + 1)
                nc.vector.tensor_scalar(rstd_tok[:], bank[:, 7, 0:NT], 1.0 / D, EPS, ALU.mult, ALU.add).then_inc(var_ready, 1)
                dve.wait_ge(root_ready, norm + 1)
                nc.vector.reciprocal(rstd_tok[:], rstd_tok[:]).then_inc(rstd_tok_ready, 1)
                if norm == 0:
                    dve.wait_ge(ident_loaded, 16)
                dve.wait_ge(rstd_tok_ready, norm + 1)
                for j in range(NT):
                    ins = nc.vector.tensor_scalar(spread[:, j, :], ident[:], rstd_tok[:, j:j + 1], None, ALU.mult)
                ins.then_inc(spread_ready, 1)
                dve.wait_ge(rstd_ready, norm + 1)

            def gate_step(f, g, i, mid, end, first=False):
                n = FFN[f, g][0]
                t = t_first(n)
                c = f * STEPS + steps_before[g]
                for m in range(2):
                    dve.wait_ge(tile_done, t + m + 5 + 4 * i)
                    if first:
                        nc.vector.tensor_copy(gate_pre[:, m, :], bank[:, (t + m) % 4, :]).then_inc(tile_taken, 1)
                    else:
                        nc.vector.tensor_tensor(gate_pre[:, m, :], bank[:, (t + m) % 4, :], rstd[:], ALU.mult)\
                          .then_inc(tile_taken, 1)
                mid()
                if first:
                    token_rstd(0)
                    dve.wait_ge(tile_taken, t + 6)
                    for m in range(2):
                        nc.vector.tensor_tensor(gate_pre[:, m, :], gate_pre[:, m, :], rstd[:], ALU.mult)\
                          .then_inc(first_scaled, 1)
                for m in range(2):
                    dve.wait_ge(silu_scaled, (c + i) * 2 + m + 1)
                    dve.wait_ge(tile_done, t + 2 + m + 5 + 4 * i)
                    nc.vector.tensor_tensor(hid[:, m, :], bank[:, (t + 2 + m) % 4, :], gate_act[:, m, :], ALU.mult)\
                      .then_inc(tile_taken, 1)
                    to = bass.ds(i * 2 + m, 1) if not isinstance(i, int) else slice(2 * i + m, 2 * i + m + 1)
                    dve.wait_ge(tile_taken, t + 2 + m + 5 + 4 * i)
                    nc.vector.tensor_scalar(h_hi[:, to, :], hid[:, m:m + 1, :], 1.0, None, ALU.mult)\
                      .then_inc(h_hi_ready, 1)
                    dve.wait_ge(h_hi_ready, (c + i) * 2 + m + 1)
                    nc.vector.tensor_tensor(h_lo[:, to, :], hid[:, m:m + 1, :], h_hi[:, to, :].bitcast(F32),
                                            ALU.subtract).then_inc(h_ready, 1)
                end()

            def add_residual(n, m, k, factor):
                t = t_first(n) + m
                dve.wait_ge(tile_done, t + 5)
                nc.vector.scalar_tensor_tensor(xT[:, k, :], bank[:, t % 4, :], factor, xT[:, k, :],
                                               ALU.mult, ALU.add).then_inc(tile_taken, 1)

            def ffn(f):
                for g, hidden in enumerate(GROUPS):
                    n, nd = FFN[f, g]
                    s0 = 0
                    if g == 0 and f == 0:
                        gate_step(0, 0, 0, lambda: split(2), lambda: split(3), first=True)
                        dve.wait_ge(low_hi_ready, 1)
                        dve.wait_ge(small_loaded, 48)
                        nc.vector.tensor_tensor(low_split[:, :, 1, :], low_raw[:], low_split[:, :, 0, :].bitcast(F32),
                                                ALU.subtract).then_inc(low_lo_ready, 1)
                        s0 = 1
                    elif g == 0:
                        token_rstd(2)
                    with dve.Fori(s0, hidden // 2 - 1) as i:
                        gate_step(f, g, i, lambda: split(n + 2, i), lambda: split(n + 3, i))
                    gate_step(f, g, hidden // 2 - 1, lambda: split(nd), lambda: split(nd + 1))
                    for j in range(D // PW):
                        if nd + j == NPANELS - 1:
                            break
                        for m in range(2):
                            add_residual(nd + j, m, 2 * j + m, 0.5)
                            if g == len(GROUPS) - 1 and f == 0:
                                gain_lo(1, 2 * j + m)
                        if nd + j + 2 < NPANELS and nd + j + 2 != PN[GQ]:
                            split(nd + j + 2)

            for c, (k0, k1) in enumerate(CHUNKS):
                last = c == len(CHUNKS) - 1
                cols = slice(k0 * PW, k1 * PW)
                for k in range(k0, k1):
                    gain_lo(0, k)
                dve.wait_ge(hi_ready if last else hi_part, 1 if last else c + 1)
                nc.vector.tensor_tensor(w_lo[:, 0, cols], w_raw[:, 0, cols], w_hi[:, 0, cols].bitcast(F32),
                                        ALU.subtract).then_inc(lo_ready if last else lo_part, 1)
            for c, (k0, k1) in enumerate(UP_CHUNKS):
                cols = slice(k0 * PW, k1 * PW)
                dve.wait_ge(hi_ready if c else hi_part, 2 if c else len(CHUNKS))
                nc.vector.tensor_tensor(w_lo[:, 1, cols], w_raw[:, 1, cols], w_hi[:, 1, cols].bitcast(F32),
                                        ALU.subtract).then_inc(lo_ready if c else lo_part, 1)
            ffn(0)

            def take(n, m, out, factor=None):
                t = t_first(n) + m
                dve.wait_ge(tile_done, t + 5)
                if factor is None:
                    ins = nc.vector.tensor_tensor(out, bank[0:out.shape[0], t % 4, :], rstd[0:out.shape[0], :], ALU.mult)
                else:
                    ins = nc.vector.scalar_tensor_tensor(out, bank[:, t % 4, :], factor, rstd[:], ALU.mult, ALU.mult)
                ins.then_inc(tile_taken, 1)

            def rotate(q, c):
                dve.wait_ge(swap_ready, c + 1)
                nc.vector.tensor_tensor(r_qk[:, c, :], r_qk[:, c, :], rotary[:, 0, :], ALU.mult).then_inc(cos_part, 1)
                nc.vector.tensor_tensor(swapped[:, c % 2, :], swapped[:, c % 2, :], rotary[:, 1, :], ALU.mult)\
                  .then_inc(sin_part, 1)
                dve.wait_ge(cos_part, c + 1)
                dve.wait_ge(sin_part, c + 1)
                nc.vector.tensor_tensor(r_qk[:, c, :], r_qk[:, c, :], swapped[:, c % 2, :], ALU.add).then_inc(rot_ready, 1)

            def sums(level):
                s = LEVELS[level - 1]
                pre, suf = (z[:].rearrange("p a t -> p (a t)").rearrange("p (b o s) -> p b o s", o=2, s=s)
                            for z in (pre_sum, suf_sum))
                nb = 2 * T // (2 * s)
                dve.wait_ge(dec_ready, 2 * level)
                dve.wait_ge(sums_ready, level)
                nc.vector.tensor_tensor(suf[:, :, 0, :], suf[:, :, 0, :],
                                        pre[:, :, 1, s - 1:s].to_broadcast([P, nb, s]), ALU.add).then_inc(suf_ready, 1)
                dve.wait_ge(suf_ready, level)
                nc.vector.tensor_tensor(pre[:, :, 1, :], pre[:, :, 1, :],
                                        pre[:, :, 0, s - 1:s].to_broadcast([P, nb, s]), ALU.add).then_inc(sums_ready, 1)

            def queries(level):
                dve.wait_ge(dec_ready, 2 * (level + 1))
                if level == 0:
                    dve.wait_ge(tile_taken, t_end(PN[GQ]) + 4)
                if level >= 2:
                    dve.wait_ge(level_done, HEADS * (level - 1))
                nc.vector.tensor_tensor(qk_dec[:, level % 2, 0, :], g_qk[:, 0:2, :].rearrange("p a t -> p (a t)"),
                                        dec[:].rearrange("p a t -> p (a t)"), ALU.mult).then_inc(q_dec_ready, 1)

            def take_same():
                dve.wait_ge(same_done, 1)
                nc.vector.tensor_copy(same[:].rearrange("p j h -> p (j h)"), bank[:, 7, 0:NT * HEADS]).then_inc(same_taken, 1)

            def put_same():
                dve.wait_ge(same_taken, 1)
                dve.wait_ge(av_done, NT)
                for h in range(HEADS):
                    ins = nc.vector.tensor_tensor(g_diag[:, h], ident[:].rearrange("p (o c) -> p o c", o=1).to_broadcast([P, NT, P]),
                                                  same[:, :, h:h + 1].to_broadcast([P, NT, P]), ALU.mult)
                ins.then_inc(same_ready, 1)

            def select(level):
                if level == 0:
                    dve.wait_ge(same_ready, 1)
                for h in range(HEADS):
                    dve.wait_ge(level_done, HEADS * level + h + 1)
                    if level < NMASK:
                        nc.vector.copy_predicated(g_diag[:, h], masks[:, level:level + 1, :].to_broadcast([P, NT, P]),
                                                  bank[:, 4 + h, :].rearrange("p (j c) -> p j c", j=NT))\
                          .then_inc(level_taken, 1)
                    else:
                        nc.vector.tensor_copy(g_diag[0:CHUNK, h, :, CHUNK:P],
                                              bank[0:CHUNK, 4 + h, :].rearrange("p (j c) -> p j c", j=NT)[:, :, CHUNK:P])\
                          .then_inc(level_taken, 1)

            def means(grp, j):
                c = NT * grp + j
                dve.wait_ge(av_squared, c + 1)
                nc.vector.reduce_sum(head_ms[:, grp, j, :], sq[:].rearrange("p (h c) -> p h c", h=HEADS),
                                     AX.X).then_inc(sq_reduced, 1)
                if j < NT - 1:
                    return
                ms = head_ms[:, grp]
                dve.wait_ge(sq_reduced, c + 1)
                nc.vector.tensor_scalar(ms, ms, 1.0 / DV, EPS, ALU.mult, ALU.add).then_inc(hvar_ready, 1)
                dve.wait_ge(hroot_ready, grp + 1)
                nc.vector.reciprocal(ms, ms).then_inc(hrstd_ready, 1)
                dve.wait_ge(hrstd_ready, grp + 1)
                for i in range(NT):
                    nc.vector.tensor_tensor(o_tok[grp][:, i, :].rearrange("p (h c) -> p h c", h=HEADS),
                                            bank[:, 4 + i, :].rearrange("p (h c) -> p h c", h=HEADS),
                                            head_ms[:, grp, i, :].rearrange("p (h o) -> p h o", o=1).to_broadcast([P, HEADS, DV]),
                                            ALU.mult).then_inc(o_normed, 1)

            def gate_take(n, *tiles):
                for m in tiles or range(2):
                    h = t_first(n) + m - t_first(PN[RG])
                    if h == 0:
                        dve.wait_ge(rs_done, HEADS * NT)
                    if h >= 4:
                        dve.wait_ge(o_gated, h - 3)
                    take(n, m, r_qk[:, h % 4, :])

            def gate_mul(n, *tiles):
                for m in tiles or range(2):
                    h = t_first(n) + m - t_first(PN[RG])
                    dve.wait_ge(gate_silu, h + 1)
                    if h < HEADS:
                        dve.wait_ge(o_copied, h + 1)
                        o = o_T[:, h, :]
                    else:
                        dve.wait_ge(o_turned, h + 1)
                        o = bank[:, 4 + h - HEADS, :]
                    nc.vector.scalar_tensor_tensor(o_T[:, h, :], o, gains[:, 4, h:h + 1],
                                                   r_qk[:, h % 4, :], ALU.mult, ALU.mult).then_inc(o_gated, 1)

            def heads_lo(*heads):
                for h in heads:
                    dve.wait_ge(heads_hi_ready, h + 1)
                    nc.vector.tensor_tensor(h_lo[:, h, :], o_T[:, h, :], h_hi[:, head_slot(h), :].bitcast(F32), ALU.subtract)\
                      .then_inc(heads_lo_ready, 1)

            token_rstd(1)
            dve.wait_ge(low_done, 1)
            nc.vector.tensor_tensor(low[:], bank[0:2 * RANK, 5, :], rstd[0:2 * RANK, :], ALU.mult).then_inc(low_taken, 1)
            split(PN[GQ])
            take(PN[GK], 0, g_qk[:, 2, :])
            take(PN[GK], 1, g_qk[:, 3, :])
            nc.vector.memset(suf_sum[:], 0.0)
            for b in range(2):
                dve.wait_ge(logits_done, b + 1)
                nc.vector.tensor_scalar(pre_sum[:, b, :], bank[:, 4 + b, :], gate_bias[:, b:b + 1], None, ALU.add)\
                  .then_inc(logit_ready, 1)
            split(PN[RQ])
            dve.wait_ge(logit_ln, 1)
            nc.vector.scalar_tensor_tensor(pre_sum[:].rearrange("p a t -> p (a t)"), pre_sum[:].rearrange("p a t -> p (a t)"),
                                           0.0, dec[:].rearrange("p a t -> p (a t)"), ALU.min, ALU.subtract)\
              .then_inc(sums_ready, 1)
            take(PN[GQ], 0, g_qk[:, 0, :], DK ** -0.5)
            take(PN[GQ], 1, g_qk[:, 1, :], DK ** -0.5)
            queries(0)
            split(PN[RK])
            sums(1)
            take(PN[RQ], 0, r_qk[:, 0, :])
            take(PN[RQ], 1, r_qk[:, 1, :])
            split(PN[RV])
            rotate(PN[RQ], 0)
            rotate(PN[RQ], 1)
            take(PN[RK], 0, r_qk[:, 2, :])
            take(PN[RK], 1, r_qk[:, 3, :])
            rotate(PN[RK], 2)
            split(PN[RV + 1])
            rotate(PN[RK], 3)

            def take_v(n, grp, part, *tiles):
                for m in tiles or range(2):
                    t = t_first(n) + m
                    dve.wait_ge(tile_done, t + 5)
                    for b in range(2):
                        j = 2 * m + b
                        ins = nc.vector.tensor_scalar(v_tok[:, grp, j, PW * part:PW * part + PW],
                                                      bank[:, t % 4, PW * b:PW * b + PW], rstd_tok[:, j:j + 1], None, ALU.mult)
                    ins.then_inc(tile_taken, 1)

            def decay_scores(*heads):
                for h in heads:
                    for j in range(NT):
                        w = T - P * j
                        dve.wait_ge(rs_done, NT * h + j + 1)
                        nc.vector.tensor_tensor(r_scores[:, h, SCORE_AT[j]:SCORE_AT[j] + w], bank[:, 4 + j, 0:w],
                                                r_decay[:, h, 0:w], ALU.mult).then_inc(rs_taken, 1)

            take_v(PN[RV], 0, 0)
            dve.wait_ge(decay_loaded, 16)
            dve.wait_ge(masks_ready, 1)
            decay_scores(0, 1)
            take_v(PN[RV + 1], 0, 1, 0)
            split(PN[GV])
            decay_scores(2, 3)
            take_v(PN[RV + 1], 0, 1, 1)
            queries(1)
            sums(2)
            split(PN[GV + 1])
            take_v(PN[GV], 1, 0, 0)
            take_same()
            for j in range(NT):
                means(0, j)
            take_v(PN[GV], 1, 0, 1)
            split(PN[RG])
            take_v(PN[GV + 1], 1, 1, 0)
            put_same()
            take_v(PN[GV + 1], 1, 1, 1)
            split(PN[RG + 1])
            for level, then in ((0, lambda: gate_take(PN[RG], 0)),
                                (1, lambda: (gate_take(PN[RG], 1), split(PN[GG]))),
                                (2, lambda: gate_take(PN[RG + 1], 0)),
                                (3, lambda: (gate_take(PN[RG + 1], 1), split(PN[GG + 1]))),
                                (4, lambda: (gate_mul(PN[RG]), gate_mul(PN[RG + 1]), gate_take(PN[GG], 0))),
                                (5, lambda: (gate_take(PN[GG], 1), split(WOUT))),
                                (6, lambda: gate_take(PN[GG + 1], 0))):
                select(level)
                queries(level + 2)
                if level + 3 < len(LEVELS):
                    sums(level + 3)
                then()
            for j in range(NT):
                means(1, j)
            gate_take(PN[GG + 1], 1)
            gate_mul(PN[GG])
            gate_mul(PN[GG + 1])
            heads_lo(5, 7)
            split(WOUT + 1)
            for j in range(D // PW):
                for m in range(2):
                    add_residual(WOUT + j, m, 2 * j + m, 1.0)
                    gain_lo(2, 2 * j + m)
                split(WOUT + j + 2)
            ffn(1)

            def add_half(half, m):
                t = t_first(NPANELS - 1) + m
                k = KD - 2 + m
                cols = slice(half * HALF, half * HALF + HALF)
                dve.wait_ge(half_done, 2 * half + m + 1)
                nc.vector.scalar_tensor_tensor(xT[:, k, cols], bank[:, (t + 2 * half) % 4, cols], 0.5, xT[:, k, cols],
                                               ALU.mult, ALU.add).then_inc(half_added, 1)

            def half_recip(half):
                mine = rstd_tok[:, 2 * half:2 * half + 2]
                dve.wait_ge(half_root, half + 1)
                nc.vector.reciprocal(mine, mine).then_inc(half_rstd, 1)
                dve.wait_ge(half_rstd, half + 1)
                for j in (2 * half, 2 * half + 1):
                    ins = nc.vector.tensor_scalar(spread[:, j, :], ident[:], rstd_tok[:, j:j + 1], None, ALU.mult)
                ins.then_inc(half_spread, 1)

            def out_half(half, *tiles):
                cols = slice(half * HALF, half * HALF + HALF)
                dve.wait_ge(half_ready, half + 1)
                for k in tiles:
                    nc.vector.scalar_tensor_tensor(xT[:, k, cols], xT[:, k, cols], gains[:, 3, k:k + 1],
                                                   bank[:, 4 + half, 0:HALF], ALU.mult, ALU.mult).then_inc(out_ready, 1)

            add_half(0, 0)
            add_half(0, 1)
            add_half(1, 0)
            half_recip(0)
            out_half(0, 0, 1)
            add_half(1, 1)
            out_half(0, 2, 3, 4)
            half_recip(1)
            out_half(0, 5, 6, 7)
            out_half(1, *range(KD))

        @block.tensor
        def _(pe):
            pe.sem_inc(tile_done, 4)
            pe.wait_ge(ones_ready, 1)
            for _ in range(WARM_UP):
                nc.tensor.matmul(bank[:, 7, 0:P], ones[:], ones[:], start=True, stop=True)

            def tile(n, m, kt, hi, lo, fresh=None, i=0, hi_at=lambda k: k):
                t = t_first(n) + m
                pe.wait_ge(tile_taken, t + 1 + 4 * i)
                out = bank[:, t % 4, :]
                for k in range(kt):
                    at = k * PW + m * P
                    if fresh is not None:
                        pe.wait_ge(*fresh(k))
                    wh, wl = (w[:, n % 2, at:at + P] for w in (w_hi, w_lo))
                    nc.tensor.matmul(out, wh, hi[:, hi_at(k), :], start=(k == 0), stop=False)
                    nc.tensor.matmul(out, wh, lo[:, k, :], start=False, stop=False)
                    ins = nc.tensor.matmul(out, wl, hi[:, hi_at(k), :], start=False, stop=(k == kt - 1))
                ins.then_inc(tile_done, 1)

            def mean_square(norm):
                pe.wait_ge(sum_ready, KD * (norm + 1))
                for j in range(NT):
                    c = slice(P * j, P * j + P)
                    ins = nc.tensor.matmul(bank[:, 7, j:j + 1], sq_sum[:, c], ones[:, 0:1], start=True, stop=True)
                ins.then_inc(ms_done, 1)

            def spread_rstd(norm):
                pe.wait_ge(spread_ready, norm + 1)
                nc.tensor.matmul(bank[:, 6, :], ones[:], spread[:].rearrange("p j c -> p (j c)"),
                                 start=True, stop=True).then_inc(spread_done, 1)

            def panel(n, kt=KD, i=0, hi=xg_hi, lo=xg_lo, fresh=None, after_first=None, hi_at=lambda k: k):
                pe.wait_ge(lo_ready, n + 3 + 2 * i)
                tile(n, 0, kt, hi, lo, fresh=fresh, i=i, hi_at=hi_at)
                if after_first:
                    after_first()
                tile(n, 1, kt, hi, lo, i=i, hi_at=hi_at)

            def first_step():
                pe.wait_ge(tile_taken, 4)
                for c, (k0, k1) in enumerate(CHUNKS):
                    last = c == len(CHUNKS) - 1
                    pe.wait_ge(lo_ready if last else lo_part, 3 if last else c + 1)
                    for k in range(k0, k1):
                        pe.wait_ge(xg_lo_ready, k + 1)
                        for m in range(2):
                            at = k * PW + m * P
                            wh, wl = (w[:, 0, at:at + P] for w in (w_hi, w_lo))
                            nc.tensor.matmul(bank[:, m, :], wh, xg_hi[:, k, :], start=(k == 0), stop=False)
                            nc.tensor.matmul(bank[:, m, :], wh, xg_lo[:, k, :], start=False, stop=False)
                            ins = nc.tensor.matmul(bank[:, m, :], wl, xg_hi[:, k, :], start=False, stop=(k == KD - 1))
                            if k == KD - 1:
                                ins.then_inc(tile_done, 1)
                tile(1, 0, KD, xg_hi, xg_lo, fresh=lambda k: (lo_part, len(CHUNKS)) if k < UP_CHUNKS[1][0] else (lo_ready, 4))
                mean_square(0)
                tile(1, 1, KD, xg_hi, xg_lo)
                spread_rstd(0)

            def down(n, kt, fresh, hi_at=lambda k: k):
                panel(n, kt, hi=h_hi, lo=h_lo, fresh=fresh, hi_at=hi_at)
                panel(n + 1, kt, hi=h_hi, lo=h_lo, hi_at=hi_at)
                with pe.Fori(1, D // PW // 2) as i:
                    panel(n, kt, i=i, hi=h_hi, lo=h_lo, hi_at=hi_at)
                    panel(n + 1, kt, i=i, hi=h_hi, lo=h_lo, hi_at=hi_at)

            def last_panel(n, kt):
                pe.wait_ge(lo_ready, n + 3)
                for half in range(2):
                    cols = slice(half * HALF, half * HALF + HALF)
                    for m in range(2):
                        t = t_first(n) + m
                        pe.wait_ge(tile_taken, t + 1 + 2 * half)
                        out = bank[:, (t + 2 * half) % 4, cols]
                        for k in range(kt):
                            if half == 1 and m == 1 and k == SPREAD_AT:
                                half_rstd_spread(0)
                            at = k * PW + m * P
                            wh, wl = (w[:, n % 2, at:at + P] for w in (w_hi, w_lo))
                            nc.tensor.matmul(out, wh, h_hi[:, k, cols], start=(k == 0), stop=False)
                            nc.tensor.matmul(out, wh, h_lo[:, k, cols], start=False, stop=False)
                            ins = nc.tensor.matmul(out, wl, h_hi[:, k, cols], start=False, stop=(k == kt - 1))
                        ins.then_inc(half_done, 1)
                        if half == 1 and m == 0:
                            half_mean(0)
                half_mean(1)
                half_rstd_spread(1)

            def half_mean(half):
                mine = (2 * half, 2 * half + 1)
                pe.wait_ge(half_sum, half + 1)
                for j in mine:
                    nc.tensor.matmul(bank[:, 6 + j % 2, half:half + 1], sq_sum[:, P * j:P * j + P], ones[:, 0:1], start=True, stop=False)
                pe.wait_ge(half_last_sq, half + 1)
                for j in mine:
                    ins = nc.tensor.matmul(bank[:, 6 + j % 2, half:half + 1], sq_last[:, P * j:P * j + P], ones[:, 0:1], start=False, stop=True)
                ins.then_inc(half_ms, 1)

            def half_rstd_spread(half):
                pe.wait_ge(half_spread, half + 1)
                nc.tensor.matmul(bank[:, 4 + half, 0:HALF], ones[:],
                                 spread[:, 2 * half:2 * half + 2, :].rearrange("p j c -> p (j c)"),
                                 start=True, stop=True).then_inc(half_ready, 1)

            def ffn(f):
                for g, hidden in enumerate(GROUPS):
                    n, nd = FFN[f, g]
                    s0 = 0
                    if g == 0:
                        if f == 0:
                            first_step()
                        else:
                            panel(n, fresh=lambda k: (xg_lo_ready, XG[2] + k + 1), after_first=lambda: mean_square(2))
                            spread_rstd(2)
                            panel(n + 1)
                        s0 = 1
                    with pe.Fori(s0, hidden // 2) as i:
                        panel(n, i=i)
                        panel(n + 1, i=i)
                    h_there = lambda k: (h_ready, 2 * (f * STEPS + steps_before[g]) + k + 1)
                    if nd + D // PW < NPANELS:
                        down(nd, hidden, h_there)
                    else:
                        for j in range(D // PW - 1):
                            panel(nd + j, hidden, hi=h_hi, lo=h_lo, fresh=None if j else h_there)
                        last_panel(nd + D // PW - 1, hidden)

            ffn(0)

            def panel_v(n, *tiles):
                pe.wait_ge(lo_ready, n + 3)
                for m in tiles or range(2):
                    t = t_first(n) + m
                    pe.wait_ge(tile_taken, t + 1)
                    for b in range(2):
                        tok = slice(P * (2 * m + b), P * (2 * m + b) + P)
                        out = bank[:, t % 4, PW * b:PW * b + PW]
                        for k in range(KD):
                            wh, wl = (w[:, n % 2, k * PW:k * PW + PW] for w in (w_hi, w_lo))
                            nc.tensor.matmul(out, xg_hi[:, k, tok], wh, start=(k == 0), stop=False)
                            nc.tensor.matmul(out, xg_lo[:, k, tok], wh, start=False, stop=False)
                            ins = nc.tensor.matmul(out, xg_hi[:, k, tok], wl, start=False, stop=(k == KD - 1))
                    ins.then_inc(tile_done, 1)

            def same_scores():
                pe.wait_ge(head_rows_ready, 4)
                pe.wait_ge(qk_ready, 1)
                pe.wait_ge(rs_taken, HEADS * NT)
                for j in range(NT):
                    for pair in range(HEADS // 2):
                        at = HEADS * j + 2 * pair
                        ins = nc.tensor.matmul(bank[:, 7, at:at + 2], qk_same[:, pair, P * j:P * j + P], head_rows[:],
                                               start=True, stop=True)
                ins.then_inc(same_done, 1)

            def level_scores(level):
                pe.wait_ge(q_dec_ready, level + 1)
                pe.wait_ge(k_dec_ready, level + 1)
                for pair in range(HEADS // 2):
                    if level:
                        pe.wait_ge(level_taken, HEADS * (level - 1) + 2 * pair + 2)
                    q, k = (qk_dec[:, level % 2, z, T * pair:T * pair + T] for z in range(2))
                    for j in range(NT):
                        for h in (2 * pair, 2 * pair + 1):
                            rows = slice(DK * (h % 2), DK * (h % 2) + DK)
                            if level < NMASK:
                                c = slice(P * j, P * j + P)
                                ins = nc.tensor.matmul(bank[:, 4 + h, c], k[rows, c], q[rows, c], start=True, stop=True)
                            else:
                                kc, qc = slice(P * j, P * j + CHUNK), slice(P * j + CHUNK, P * j + P)
                                ins = nc.tensor.matmul(bank[0:CHUNK, 4 + h, qc], k[rows, kc], q[rows, qc], start=True, stop=True)
                            if j == NT - 1:
                                ins.then_inc(level_done, 1)

            def far_scores(level):
                pe.wait_ge(q_dec_ready, level + 1)
                pe.wait_ge(k_dec_ready, level + 1)
                blocks = ((0, P, 2 * P), (2 * P, 3 * P, 4 * P)) if level == 7 else ((0, 2 * P, 4 * P), (P, 2 * P, 4 * P))
                for pair in range(HEADS // 2):
                    if level == 7:
                        pe.wait_ge(level_taken, HEADS * (DIAG_LEVELS - 1) + 2 * pair + 2)
                    else:
                        pe.wait_ge(far_taken, 2 * pair + 2)
                    q, k = (qk_dec[:, level % 2, z, T * pair:T * pair + T] for z in range(2))
                    at = 0
                    for b, (j0, i0, i1) in enumerate(blocks):
                        for h in (2 * pair, 2 * pair + 1):
                            rows = slice(DK * (h % 2), DK * (h % 2) + DK)
                            ins = nc.tensor.matmul(bank[:, 4 + h, at:at + i1 - i0], k[rows, j0:j0 + P], q[rows, i0:i1],
                                                   start=True, stop=True)
                            if b == len(blocks) - 1:
                                ins.then_inc(far_done, 1)
                        at += i1 - i0

            def retention_scores(h):
                rows = slice(DK * (h % 2), DK * (h % 2) + DK)
                for j in range(NT):
                    if h:
                        pe.wait_ge(rs_taken, NT * (h - 1) + j + 1)
                    nc.tensor.matmul(bank[:, 4 + j, 0:T - P * j], r_qk[rows, 2 + h // 2, P * j:P * j + P],
                                     r_qk[rows, h // 2, P * j:T], start=True, stop=True).then_inc(rs_done, 1)

            def outputs(grp, i):
                if grp:
                    pe.wait_ge(level_taken, HEADS * DIAG_LEVELS)
                    pe.wait_ge(far_taken, 2 * HEADS if i > 1 else HEADS + i + 1)
                else:
                    if i == NT - 1:
                        pe.wait_ge(same_taken, 1)
                    pe.wait_ge(rs_taken, HEADS * NT)
                    pe.wait_ge(tile_taken, t_end(PN[RV + 1]) + 4)
                for h in range(HEADS):
                    for j in range(i + 1):
                        if grp == 0:
                            at = SCORE_AT[j] + P * (i - j)
                            score = r_scores[:, h, at:at + P]
                        elif i == j:
                            score = g_diag[:, h, j, :]
                        else:
                            at = (0, 3 * P, 5 * P)[j] + P * (i - j - 1)
                            score = g_off[:, h, at:at + P]
                        ins = nc.tensor.matmul(bank[:, 4 + i, DV * h:DV * h + DV], score,
                                               v_tok[:, grp, j, DV * h:DV * h + DV], start=(j == 0), stop=(j == i))
                ins.then_inc(av_done, 1)

            def turn(grp):
                pe.wait_ge(o_normed, NT * (grp + 1))
                for h in range(HEADS):
                    for i in range(NT):
                        ins = nc.tensor.transpose(bank[:, 4 + h, P * i:P * i + P], o_tok[grp][:, i, DV * h:DV * h + DV],
                                                  ident[:])
                    ins.then_inc(o_turned, 1)

            pe.wait_ge(low_lo_ready, 1)
            for k in range(KD):
                pe.wait_ge(xg_lo_ready, XG[1] + k + 1)
                w = low_split[:, k, :, :].rearrange("p z c -> p (z c)")
                nc.tensor.matmul(bank[0:2 * RANK, 5, :], w, xg_hi[:, k, :], start=(k == 0), stop=False)
                ins = nc.tensor.matmul(bank[0:2 * RANK, 5, :], w, xg_lo[:, k, :], start=False, stop=(k == KD - 1))
            ins.then_inc(low_done, 1)
            mean_square(1)
            panel(PN[GK], after_first=lambda: spread_rstd(1))
            pe.wait_ge(low_taken, 1)
            for b in range(2):
                nc.tensor.matmul(bank[:, 4 + b, :], a2[:, P * b:P * b + P], low[:], start=True, stop=True)\
                  .then_inc(logits_done, 1)
            panel(PN[GQ])
            panel(PN[RQ])
            panel(PN[RK])
            panel_v(PN[RV])
            panel_v(PN[RV + 1], 0)
            pe.wait_ge(rot_ready, 4)
            pe.wait_ge(logit_ready, 2)
            pe.wait_ge(rstd_ready, 2)
            retention_scores(0)
            retention_scores(1)
            panel_v(PN[RV + 1], 1)
            retention_scores(2)
            retention_scores(3)
            panel_v(PN[GV], 0)
            same_scores()
            for i in range(NT):
                outputs(0, i)
            panel_v(PN[GV], 1)
            turn(0)
            panel_v(PN[GV + 1], 0)
            panel_v(PN[GV + 1], 1)
            pe.wait_ge(o_copied, HEADS)
            for level, (n, m) in enumerate((n, m) for n in (PN[RG], PN[RG + 1], PN[GG], PN[GG + 1]) for m in range(2)):
                if level < DIAG_LEVELS:
                    level_scores(level)
                else:
                    far_scores(7)
                    far_scores(8)
                    for i in range(NT):
                        outputs(1, i)
                pe.wait_ge(lo_ready, n + 3)
                tile(n, m, KD, xg_hi, xg_lo)
            turn(1)
            down(WOUT, KD, lambda k: {5: (heads_lo_ready, 1), 6: (pool_lo_ready, 6), 7: (heads_lo_ready, 2)}
                 .get(k, (pool_lo_ready, k + 1)), hi_at=head_slot)
            ffn(1)


def kernel(x, ffn1_norm_g, ffn1_w_gate, ffn1_w_up, ffn1_w_down, mix_norm_g, w_in, ret_norm_g, gla_w_a2, gla_b_a,
           gla_norm_g, w_out, ffn2_norm_g, ffn2_w_gate, ffn2_w_up, ffn2_w_down, final_norm_g):
    import concourse.bacc as bacc
    from concourse.bass_utils import run_bass_kernel_spmd

    def row_tiles(w):
        w = np.asarray(w)
        rows, cols = w.shape
        w = w.reshape(rows // P, P, cols // PW, PW).transpose(2, 1, 0, 3)
        return np.ascontiguousarray(w).reshape(cols // PW, P, rows // P * PW)

    def columns(v):
        return np.asarray(v).reshape(-1, P).T

    w_in = np.asarray(w_in)[0]
    wide = w_in.shape[1] - RANK
    rotary, decay, masks = tables()
    heads_g = np.concatenate([np.asarray(ret_norm_g)[0], np.asarray(gla_norm_g)[0]])
    arrays = {
        "x": np.ascontiguousarray(np.asarray(x)[0].T.reshape(KD, P, T).transpose(1, 0, 2)),
        "gate0": row_tiles(ffn1_w_gate[0]), "up0": row_tiles(ffn1_w_up[0]), "down0": row_tiles(ffn1_w_down[0]),
        "gate1": row_tiles(ffn2_w_gate[0]), "up1": row_tiles(ffn2_w_up[0]), "down1": row_tiles(ffn2_w_down[0]),
        "w_in": row_tiles(w_in[:, :wide]), "w_out": row_tiles(w_out[0]),
        "w_low": np.ascontiguousarray(w_in[:, wide:].reshape(KD, P, RANK).transpose(1, 0, 2)),
        "gains": np.ascontiguousarray(np.stack([columns(g) for g in (
            np.asarray(ffn1_norm_g)[0], np.asarray(mix_norm_g)[0], np.asarray(ffn2_norm_g)[0],
            final_norm_g, heads_g)], axis=1)),
        "a2": np.concatenate([np.asarray(gla_w_a2)[0]] * 2),
        "gate_bias": np.ascontiguousarray(columns(np.asarray(gla_b_a)[0])),
        "ident": np.eye(P, dtype=np.float32), "rotary": rotary, "decay": decay, "masks": masks,
    }
    nc = bacc.Bacc("TRN2", target_bir_lowering=False, num_devices=1)
    handles = {n: nc.dram_tensor("in_" + n, v.shape, mybir.dt.from_np(v.dtype), kind="ExternalInput").ap()
               for n, v in arrays.items()}
    handles["out"] = nc.dram_tensor("out_xT", (P, KD, T), F32, kind="ExternalOutput").ap()
    build(nc, handles)
    r = run_bass_kernel_spmd(nc, [{"in_" + n: v for n, v in arrays.items()}], core_ids=[0])
    out = r.results[0]["out_xT"]
    return np.ascontiguousarray(out.transpose(2, 1, 0).reshape(1, T, D))
```
